# Optimizing a Trainium2 kernel written in Bass

```python
import jax, jax.numpy as jnp
from jax import lax
import numpy as np

D_MODEL = 2048
BATCH = 1
SEQ = 128
DEPTH = 2
DEC_BATCH = 1
DEC_SEQ = 128
PAST_LEN = 128

GRID_W = 64
HEAD_DIM = 128
CONV_CH = 512
CONV_WIDTH = 31
GLOB_HEADS = 6
GLOB_KV = 2
WIN_HEADS = 6
WIN_KV = 2
WINDOW = 128
Q_BLOCK = 128
D_FF = 4 * D_MODEL
ROPE_THETA = 10000.0
NORM_EPS = 1e-6
NEG_INF = -1e30

GLOB_Q = GLOB_HEADS * HEAD_DIM
GLOB_KVW = GLOB_KV * HEAD_DIM
WIN_Q = WIN_HEADS * HEAD_DIM
WIN_KVW = WIN_KV * HEAD_DIM
MIX_WIDTH = CONV_CH + GLOB_Q + WIN_Q
IN_WIDTH = 2 * CONV_CH + GLOB_Q + 2 * GLOB_KVW + WIN_Q + 2 * WIN_KVW
IN_SPLITS = tuple(int(v) for v in np.cumsum(
    [2 * CONV_CH, GLOB_Q, GLOB_KVW, GLOB_KVW, WIN_Q, WIN_KVW])[:])

kernel_name = 'hybrid_dit_conv_gqa_swa_step'

def rms_norm(x, g):
    xf = x.astype(jnp.float32)
    y = xf * lax.rsqrt(jnp.mean(xf * xf, axis=-1, keepdims=True) + NORM_EPS)
    return (y * g.astype(jnp.float32)).astype(x.dtype)

def layer_norm(x, g, b):
    xf = x.astype(jnp.float32)
    mu = jnp.mean(xf, axis=-1, keepdims=True)
    var = jnp.mean(jnp.square(xf - mu), axis=-1, keepdims=True)
    y = (xf - mu) * lax.rsqrt(var + NORM_EPS)
    return (y * g.astype(jnp.float32) + b.astype(jnp.float32)).astype(x.dtype)

def axial_rope_tables(n_tokens):
    rows = n_tokens // GRID_W
    r, col = jnp.meshgrid(jnp.arange(rows), jnp.arange(GRID_W), indexing='ij')
    r = r.reshape(-1).astype(jnp.float32)
    col = col.reshape(-1).astype(jnp.float32)
    n_freq = HEAD_DIM // 4
    inv = ROPE_THETA ** (-jnp.arange(n_freq, dtype=jnp.float32) / n_freq)
    ang_r = r[:, None] * inv
    ang_c = col[:, None] * inv
    ang = jnp.concatenate([ang_r, ang_r, ang_c, ang_c], axis=-1)
    return jnp.cos(ang), jnp.sin(ang)

def apply_rope(x, cos, sin):
    x1, x2, x3, x4 = jnp.split(x, 4, axis=-1)
    rot = jnp.concatenate([-x2, x1, -x4, x3], axis=-1)
    shape = (cos.shape[0],) + (1,) * (x.ndim - 3) + (HEAD_DIM,)
    cos = cos.reshape(shape)
    sin = sin.reshape(shape)
    return (x.astype(jnp.float32) * cos + rot.astype(jnp.float32) * sin).astype(x.dtype)

def softmax_with_sink(s, sink):
    if sink is None:
        return jax.nn.softmax(s, axis=-1)
    snk = sink.astype(jnp.float32)[None, :, :, None, None]
    m = jnp.maximum(jnp.max(s, axis=-1, keepdims=True), snk)
    e = jnp.exp(s - m)
    return e / (jnp.sum(e, axis=-1, keepdims=True) + jnp.exp(snk - m))

def block_attention(q, k, v, sink):
    B, S, KV, G, D = q.shape
    nb = S // Q_BLOCK
    scale = HEAD_DIM ** -0.5
    qb = jnp.moveaxis(q.reshape(B, nb, Q_BLOCK, KV, G, D), 1, 0)

    def one(qi):
        s = jnp.einsum('bqkgd,bskd->bkgqs', qi, k).astype(jnp.float32) * scale
        p = softmax_with_sink(s, sink).astype(v.dtype)
        return jnp.einsum('bkgqs,bskd->bqkgd', p, v)

    o = lax.map(one, qb)
    return jnp.moveaxis(o, 0, 1).reshape(B, S, KV * G * D)

def banded_attention_with_context(q, k, v, k_ctx, v_ctx, sink):
    B, L, KV, G, D = q.shape
    nb = L // Q_BLOCK
    span = Q_BLOCK + 2 * WINDOW
    n_ctx = k_ctx.shape[1]
    scale = HEAD_DIM ** -0.5
    pad = ((0, 0), (WINDOW, WINDOW), (0, 0), (0, 0))
    k_pad = jnp.pad(k, pad)
    v_pad = jnp.pad(v, pad)
    qb = jnp.moveaxis(q.reshape(B, nb, Q_BLOCK, KV, G, D), 1, 0)

    def one(args):
        qi, bi = args
        start = bi * Q_BLOCK
        kb = lax.dynamic_slice_in_dim(k_pad, start, span, axis=1)
        vb = lax.dynamic_slice_in_dim(v_pad, start, span, axis=1)
        qpos = start + jnp.arange(Q_BLOCK)
        kpos = start - WINDOW + jnp.arange(span)
        valid = ((jnp.abs(qpos[:, None] - kpos[None, :]) <= WINDOW)
                 & (kpos >= 0)[None, :] & (kpos < L)[None, :])
        s_loc = jnp.einsum('bqkgd,bskd->bkgqs', qi, kb).astype(jnp.float32) * scale
        s_loc = jnp.where(valid, s_loc, NEG_INF)
        s_ctx = jnp.einsum('bqkgd,bskd->bkgqs', qi, k_ctx).astype(jnp.float32) * scale
        p = softmax_with_sink(jnp.concatenate([s_ctx, s_loc], axis=-1), sink).astype(v.dtype)
        return (jnp.einsum('bkgqs,bskd->bqkgd', p[..., :n_ctx], v_ctx)
                + jnp.einsum('bkgqs,bskd->bqkgd', p[..., n_ctx:], vb))

    o = lax.map(one, (qb, jnp.arange(nb)))
    return jnp.moveaxis(o, 0, 1).reshape(B, L, KV * G * D)

def conv_module(u, w, b, ln_g, ln_b):
    a, gt = jnp.split(u, 2, axis=-1)
    h = a * jax.nn.sigmoid(gt)
    y = lax.conv_general_dilated(
        h, w.reshape(CONV_WIDTH, 1, CONV_CH).astype(h.dtype),
        window_strides=(1,), padding=[(CONV_WIDTH // 2, CONV_WIDTH // 2)],
        dimension_numbers=('NWC', 'WIO', 'NWC'), feature_group_count=CONV_CH)
    y = layer_norm(y + b, ln_g, ln_b)
    return jax.nn.silu(y)

def trunk_layer(x, mod, lp, ctx_kv=None, rope=None):
    shift1, scale1, gate1, shift2, scale2, gate2 = jnp.split(mod, 6, axis=-1)
    B, S, _ = x.shape
    h = rms_norm(x, lp['g_attn']) * (1 + scale1) + shift1
    proj = h @ lp['w_in']
    u_conv, q_g, k_g, v_g, q_w, k_w, v_w = jnp.split(proj, IN_SPLITS, axis=-1)
    q_g = rms_norm(q_g.reshape(B, S, GLOB_KV, GLOB_HEADS // GLOB_KV, HEAD_DIM), lp['q_norm'])
    k_g = rms_norm(k_g.reshape(B, S, GLOB_KV, HEAD_DIM), lp['k_norm'])
    v_g = v_g.reshape(B, S, GLOB_KV, HEAD_DIM)
    q_w = q_w.reshape(B, S, WIN_KV, WIN_HEADS // WIN_KV, HEAD_DIM)
    k_w = k_w.reshape(B, S, WIN_KV, HEAD_DIM)
    v_w = v_w.reshape(B, S, WIN_KV, HEAD_DIM)
    sink = lp['sink'].reshape(WIN_KV, WIN_HEADS // WIN_KV)

    y_conv = conv_module(u_conv, lp['conv_w'], lp['conv_b'], lp['conv_ln_g'], lp['conv_ln_b'])
    if ctx_kv is None:
        y_g = block_attention(q_g, k_g, v_g, None)
        y_w = block_attention(q_w, k_w, v_w, sink)
        new_kv = (k_g, v_g, k_w, v_w)
    else:
        cos, sin = rope
        ck_g, cv_g, ck_w, cv_w = ctx_kv
        q_g = apply_rope(q_g, cos, sin)
        k_g = apply_rope(k_g, cos, sin)
        y_g = block_attention(q_g, jnp.concatenate([ck_g, k_g], axis=1),
                              jnp.concatenate([cv_g, v_g], axis=1), None)
        q_w = apply_rope(q_w, cos, sin)
        k_w = apply_rope(k_w, cos, sin)
        y_w = banded_attention_with_context(q_w, k_w, v_w, ck_w, cv_w, sink)
        new_kv = None
    mix = jnp.concatenate([y_conv, y_g, y_w], axis=-1) @ lp['w_out']
    x = x + gate1 * mix
    h2 = rms_norm(x, lp['g_mlp']) * (1 + scale2) + shift2
    x = x + gate2 * (jnp.square(jax.nn.relu(h2 @ lp['w_mlp1'])) @ lp['w_mlp2'])
    return x, new_kv

def setup_inputs(seed: int = 0) -> dict:
    key = jax.random.key(seed)
    ks = jax.random.split(key, 32)
    f32 = jnp.float32
    n = lambda i, shape, s: jax.random.normal(ks[i], shape, f32) * s
    cache_g = (DEC_BATCH, DEPTH, PAST_LEN, GLOB_KV, HEAD_DIM)
    cache_w = (DEC_BATCH, DEPTH, PAST_LEN, WIN_KV, HEAD_DIM)
    return {
        'x_prompt': n(0, (BATCH, SEQ, D_MODEL), 1.0),
        'x_sample': n(1, (DEC_BATCH, DEC_SEQ, D_MODEL), 1.0),
        'cache_glob_k': n(2, cache_g, 1.0),
        'cache_glob_v': n(3, cache_g, 1.0),
        'cache_win_k': n(4, cache_w, 1.0),
        'cache_win_v': n(5, cache_w, 1.0),
        'c': n(6, (DEC_BATCH, D_MODEL), 1.0),
        'c_ctx': n(7, (D_MODEL,), 1.0),
        'w_ada': n(8, (DEPTH, D_MODEL, 6 * D_MODEL), 0.5 * D_MODEL ** -0.5),
        'b_ada': n(9, (DEPTH, 6 * D_MODEL), 0.02),
        'g_attn': 1.0 + n(10, (DEPTH, D_MODEL), 0.02),
        'g_mlp': 1.0 + n(11, (DEPTH, D_MODEL), 0.02),
        'w_in': n(12, (DEPTH, D_MODEL, IN_WIDTH), D_MODEL ** -0.5),
        'conv_w': n(13, (DEPTH, CONV_WIDTH, CONV_CH), CONV_WIDTH ** -0.5),
        'conv_b': n(14, (DEPTH, CONV_CH), 0.02),
        'conv_ln_g': 1.0 + n(15, (DEPTH, CONV_CH), 0.02),
        'conv_ln_b': n(16, (DEPTH, CONV_CH), 0.02),
        'q_norm_g': 1.0 + n(17, (DEPTH, HEAD_DIM), 0.02),
        'k_norm_g': 1.0 + n(18, (DEPTH, HEAD_DIM), 0.02),
        'sink': n(19, (DEPTH, WIN_HEADS), 0.5),
        'w_out': n(20, (DEPTH, MIX_WIDTH, D_MODEL), MIX_WIDTH ** -0.5),
        'w_mlp1': n(21, (DEPTH, D_MODEL, D_FF), D_MODEL ** -0.5),
        'w_mlp2': n(22, (DEPTH, D_FF, D_MODEL), D_FF ** -0.5),
        'g_final': 1.0 + n(23, (D_MODEL,), 0.02),
    }

def reference(x_prompt, x_sample, cache_glob_k, cache_glob_v, cache_win_k, cache_win_v,
              c, c_ctx, w_ada, b_ada, g_attn, g_mlp, w_in, conv_w, conv_b, conv_ln_g,
              conv_ln_b, q_norm_g, k_norm_g, sink, w_out, w_mlp1, w_mlp2, g_final):
    rope = axial_rope_tables(x_sample.shape[1])
    xp, xs = x_prompt, x_sample
    gk, gv, wk, wv = [], [], [], []
    for l in range(DEPTH):
        lp = {'g_attn': g_attn[l], 'g_mlp': g_mlp[l], 'w_in': w_in[l], 'conv_w': conv_w[l],
              'conv_b': conv_b[l], 'conv_ln_g': conv_ln_g[l], 'conv_ln_b': conv_ln_b[l],
              'q_norm': q_norm_g[l], 'k_norm': k_norm_g[l], 'sink': sink[l],
              'w_out': w_out[l], 'w_mlp1': w_mlp1[l], 'w_mlp2': w_mlp2[l]}
        mod_ctx = (jax.nn.silu(c_ctx) @ w_ada[l] + b_ada[l])[None, None, :]
        mod_lat = (jax.nn.silu(c) @ w_ada[l] + b_ada[l])[:, None, :]
        xp, kv = trunk_layer(xp, mod_ctx, lp)
        gk.append(kv[0]); gv.append(kv[1]); wk.append(kv[2]); wv.append(kv[3])
        ctx_kv = (cache_glob_k[:, l], cache_glob_v[:, l], cache_win_k[:, l], cache_win_v[:, l])
        xs, _ = trunk_layer(xs, mod_lat, lp, ctx_kv=ctx_kv, rope=rope)
    y_prompt = rms_norm(xp, g_final)
    y_sample = rms_norm(xs, g_final)
    new_glob_k = jnp.stack(gk, axis=1)
    new_glob_v = jnp.stack(gv, axis=1)
    new_win_k = jnp.stack(wk, axis=1)
    new_win_v = jnp.stack(wv, axis=1)
    return (y_prompt, y_sample, new_glob_k, new_glob_v, new_win_k, new_win_v)


_drawn_inputs = setup_inputs


def setup_inputs(seed=0):
    import zlib

    import numpy as np

    out = dict(_drawn_inputs(seed))
    spreads = {}
    factors = {'cache_glob_k': 3.886,
     'cache_glob_v': 3.067,
     'cache_win_k': 3.541,
     'cache_win_v': 2.909,
     'g_attn': 2.922,
     'g_mlp': 4.827,
     'conv_b': 8.0,
     'conv_ln_g': 30.106,
     'conv_ln_b': 29.945,
     'q_norm_g': 23.333,
     'k_norm_g': 2.83,
     'sink': 64.0,
     'g_final': 22.8}
    for name, (base, spread) in spreads.items():
        noise = np.random.default_rng([zlib.crc32(name.encode()), seed]).standard_normal(out[name].shape)
        drawn = base * np.exp(spread * noise) if base else spread * noise
        out[name] = __import__('jax').numpy.asarray(drawn.astype(out[name].dtype))
    for name, factor in factors.items():
        out[name] = (out[name] * factor).astype(out[name].dtype)
    return out
```

```python
import numpy as np
import concourse.bass as bass
from concourse import mybir

f32 = mybir.dt.float32
f32r = mybir.dt.float32r
ALU = mybir.AluOpType
ACT = mybir.ActivationFunctionType
AX = mybir.AxisListType

P = 128
S = 2
D = 2048
KT = D // P
TOK = S * P
DEPTH = 2
EPS = 1e-6
GRID_W = 64
CONV = 512
CT = CONV // P
TAPS = 31
HALO = TAPS // 2
HEADS = 6
KV = 2
GROUP = HEADS // KV
DFF = 4 * D
CHUNKS = DFF // D
SCALE = float(P) ** -0.5
IN1, IN2, OUT, UP, DOWN = 2, 5, 4, 4, 4
PAIRS_LAYER = IN1 + IN2 + OUT + CHUNKS * (UP + DOWN)
PAIRS = DEPTH * PAIRS_LAYER
BANKS = 6 * D // 512
MIX_STEPS = 1 + 2 * HEADS
ACT2_LAYER = MIX_STEPS + KT * CHUNKS
RES_LAYER = KT * (1 + CHUNKS)
UNROLL_K = 2

QG, KG, VG, QW, KW, VW = 0, 6, 8, 10, 16, 18
SHIFT1, SCALE1, GATE1, SHIFT2, SCALE2, GATE2 = (KT * n for n in range(6))
C_ID, C_PERM, C_COS, C_SIN, C_SEL = 0, 128, 256, 384, 512
CONSTS = 514
V_BADA, V_GATTN, V_GMLP = 0, 96, 112
V_TAP, V_CONVB = 0, 124
V_LNG, V_LNB, V_QN, V_KN, V_GF = 0, 4, 8, 9, 10
MISC = 26
AHEAD = 12
PRE_JOBS = 8
NORM_STEPS = KT * S
TAP_OPS = TAPS * CT
TAPS_PAIR = (TAPS - 1) // IN2


class Steps:

    def __init__(self, eng, sem):
        self.eng, self.sem, self.n = eng, sem, 0

    def done(self, ins):
        self.n += 1
        ins.then_inc(self.sem, 1)
        return self.n

    def wait(self, value):
        self.eng.wait_ge(self.sem, value)

    def link(self, ins):
        self.wait(self.done(ins))


def build(nc, t):
    at = [16640]

    def place(name, shape, dt, offset=None):
        size = 4 * int(np.prod(shape[1:]))
        if offset is None:
            offset = at[0]
            at[0] += (size + 31) // 32 * 32
        return nc.alloc_sbuf_tensor_at(name, list(shape), dt, offset=offset)

    xT = place("xT", [P, KT, TOK], f32)
    hs_at = at[0]
    hs = place("hs", [P, KT, 2 * TOK], f32r)
    act2_at = at[0]
    act2 = place("act2", [P, KT, 2 * TOK], f32r)
    raw = place("raw", [P, 4, 8, 256], f32)
    hi = place("hi", [P, 4, 4, 256], f32r)
    lo = place("lo", [P, 4, 4, 256], f32r)
    ada = place("ada", [P, 2, 4, 512], f32)
    zq = place("zq", [P, 20, TOK], f32)
    tmp = place("tmp", [P, 2, TOK], f32)
    tsum = place("tsum", [P, 2, TOK], f32)
    thid = place("thid", [P, 2, TOK], f32)
    rows = place("rows", [P, 512], f32)
    mods = place("mods", [P, DEPTH, 96, S], f32)
    vecs = place("vecs", [P, DEPTH, 3, P], f32)
    cst = place("cst", [P, CONSTS], f32)
    ones = place("ones", [P, P], f32)
    ssq = place("ssq", [P, TOK], f32)
    std = place("std", [P, TOK], f32)
    rstd = place("rstd", [P, TOK], f32)
    cT = place("cT", [P, KT, 32], f32)
    craw = place("craw", [P, S, KT], f32)
    csig = place("csig", [P, S, KT], f32)
    amul = place("amul", [P, KT, S], f32)
    ybuf = place("ybuf", [P, 2 * UNROLL_K, P], f32)
    sinks = place("sinks", [P, DEPTH, HEADS], f32)
    nsinks = place("nsinks", [P, DEPTH, HEADS], f32)
    eps = place("eps", [P, 1], f32)
    mx = place("mx", [P, 2 * HEADS, S], f32)
    nb = place("nb", [P, 2 * HEADS, S], f32)
    rsum = place("rsum", [P, 2 * HEADS, S], f32)
    esink = place("esink", [P, 2 * HEADS, S], f32)
    rinv = place("rinv", [P, 2 * HEADS, S], f32)
    assert at[0] <= 229368, at[0]

    xtok = place("xtok", [P, S, D], f32, hs_at)
    ktokc = place("ktokc", [P, 2 * KV, P], f32, hs_at)
    vc = place("vc", [P, 2 * KV, P], f32, hs_at + 2048)
    kcT = place("kcT", [P, 2 * KV, P], f32, hs_at + 4096)
    vtok = place("vtok", [P, S, 2 * KV, P], f32, hs_at + 6144)
    ktok = place("ktok", [P, 2 * KV, P], f32, hs_at + 10240)
    qsq = place("qsq", [P, 8, TOK], f32, hs_at + 12288)
    qrs = place("qrs", [P, 4, 512], f32, hs_at + 20480)
    rot = place("rot", [P, 2, 512], f32, hs_at + 28672)
    prob = place("prob", [P, 4, 3 * P], f32, hs_at + 12288)
    probT = place("probT", [P, 2, 3 * P], f32, hs_at + 20480)
    vrows = place("vrows", [P, DEPTH, 3, P], f32, act2_at)
    zc = place("zc", [P, 2 * CT, TOK], f32, act2_at + 8192)
    hpad = place("hpad", [P, CT, S, P + 2 * HALO], f32, act2_at + 16384)
    yconv = place("yconv", [P, CT, TOK], f32, act2_at + 21504)
    ysq = place("ysq", [P, CT, TOK], f32, act2_at + 25600)
    nmean = place("nmean", [P, TOK], f32, act2_at + 29696)
    yT = place("yT", [P, KT, TOK], f32, act2_at)
    xsq = place("xsq", [P, KT, TOK], f32, hs_at + 16384)

    pb = [nc.alloc_psum_tensor(f"bank{n}", [P, 512], f32) for n in range(8)]
    ada_ps, mod_ps = pb[4], pb[5]

    ident = cst[:, C_ID:C_ID + P]
    perm = cst[:, C_PERM:C_PERM + P]
    cosT = cst[:, C_COS:C_COS + P]
    sinT = cst[:, C_SIN:C_SIN + P]
    sel = cst[:, C_SEL:C_SEL + 2]

    def sem(name):
        return nc.alloc_semaphore(name)

    consts_in, c_in, vecs_in, sinks_in, x_in = (
        sem("consts_in"), sem("c_in"), sem("vecs_in"), sem("sinks_in"), sem("x_in"))
    raw_landed = [sem(f"raw_landed{n}") for n in range(4)]
    ada_landed = [sem(f"ada_landed{n}") for n in range(2)]
    hi_ready = sem("hi_ready")
    lo_ready = sem("lo_ready")
    half_used = sem("half_used")
    tmp_ready = sem("tmp_ready")
    bank_freed = sem("bank_freed")
    hs_ready = sem("hs_ready")
    act2_ready = sem("act2_ready")
    norm_y = sem("norm_y")
    norm_hi = sem("norm_hi")
    relu2_ready, hid_hi = sem("relu2_ready"), sem("hid_hi")
    x_updated, sq_ready, ssq_steps = sem("x_updated"), sem("sq_ready"), sem("ssq_steps")
    stat_ready, std_ready = sem("stat_ready"), sem("std_ready")
    ada_used, rows_ready = sem("ada_used"), sem("rows_ready")
    modps_ready, mods_done = sem("modps_ready"), sem("mods_done")
    dve_step = sem("dve_step")
    ones_set, eps_set, c_sig, c_ready = sem("ones_set"), sem("eps_set"), sem("c_sig"), sem("c_ready")
    vecs_turned, vecs_ready = sem("vecs_turned"), sem("vecs_ready")
    x_turned, x_ready, xsq_ready, ssq_set = sem("x_turned"), sem("x_ready"), sem("xsq_ready"), sem("ssq_set")
    cache_landed, kv_stored, y_stored = sem("cache_landed"), sem("kv_stored"), sem("y_stored")
    gate_sig, conv_tap = sem("gate_sig"), sem("conv_tap")
    conv_act, conv_dve, conv_pe = sem("conv_act"), sem("conv_dve"), sem("conv_pe")
    swap_ready, rope_done = sem("swap_ready"), sem("rope_done")
    turn_ready, turn_drained = sem("turn_ready"), sem("turn_drained")
    qsq_ready, qstat_ready, qstd_ready, qnorm_done = (
        sem("qsq_ready"), sem("qstat_ready"), sem("qstd_ready"), sem("qnorm_done"))
    score_ready, max_ready, exp_ready, prob_ready = (
        sem("score_ready"), sem("max_ready"), sem("exp_ready"), sem("prob_ready"))
    probT_ps, probT_ready, out_ready, out_hi = (
        sem("probT_ps"), sem("probT_ready"), sem("out_ready"), sem("out_hi"))
    out_turned, out_drained, yT_ready = sem("out_turned"), sem("out_drained"), sem("yT_ready")

    def walk(eng, layer, pair, stage):
        n = layer * PAIRS_LAYER
        a = layer * BANKS
        first, final = layer == 0, layer == DEPTH - 1
        a_in = a + PRE_JOBS if first else a + AHEAD
        stage("norm1", 0)
        if first:
            pair("in1", 0, 0, 0, a_in, False)
        with eng.Fori(int(first), IN1) as i:
            pair("in1", n + i, i, 0, a_in + i, False)
        stage("gate", 0)
        with eng.Fori(0, IN2) as i:
            pair("in2", n + IN1 + i, i, 0, a_in + IN1 + i, False)
        stage("attention", 0)
        n += IN1 + IN2
        stage("clear", -1)
        with eng.Fori(0, OUT) as i:
            pair("out", n + i, i, -1, a + 16 + i if first else None, False)
        stage("norm2", 0)
        n += OUT
        with eng.Fori(0, UP) as i:
            pair("up", n + i, i, 0, a + 20 + i, False)
        stage("clear", 0)
        with eng.Fori(0, DOWN) as i:
            pair("down", n + UP + i, i, 0, None, False)

        def chunk(c, end):
            m = n + (UP + DOWN) * c
            with eng.Fori(0, UP) as i:
                pair("up", m + i, i, c, a + 20 + 4 * c + i if first else None, False)
            stage("clear", c)
            with eng.Fori(0, DOWN - end) as i:
                pair("down", m + UP + i, i, c, None, False)
            if end:
                pair("down", m + UP + DOWN - 1, DOWN - 1, c, None, True)

        with eng.Fori(1, CHUNKS - final) as c:
            chunk(c, 0)
        if final:
            chunk(CHUNKS - 1, 1)

    def hidden_base(layer, c):
        return layer * ACT2_LAYER + MIX_STEPS + KT * c

    def res_tiles(layer, c):
        return layer * RES_LAYER + KT * (c + 1)

    def ssq_base(layer, c):
        return (layer * (1 + CHUNKS) + c + 1) * (1 + KT)

    def after(eng, semaphore, value):
        if not (isinstance(value, int) and value <= 0):
            eng.wait_ge(semaphore, value)

    block = nc.Block()
    with block:

        @block.sync
        def _(sp):
            sp.dma_start(craw[:, 0, :], t["c_ctx"].rearrange("(p t) -> p t", t=KT)).then_inc(c_in, 16)
            sp.dma_start(craw[:, 1, :], t["c"].rearrange("a (p t) -> (a p) t", t=KT)).then_inc(c_in, 16)
            sp.dma_start(cst[:, :], t["consts"]).then_inc(consts_in, 16)
            for s, name in enumerate(("x_prompt", "x_sample")):
                sp.dma_start(xtok[:, s, :], t[name].rearrange("a q d -> (a q) d")).then_inc(x_in, 16)
            sp.dma_start(sinks[:, :, :].rearrange("p l h -> p (l h)"),
                         t["sink"].rearrange("l h -> (l h)").partition_broadcast(P)).then_inc(sinks_in, 16)
            for l in range(DEPTH):
                for b, r, src in (
                    (0, V_BADA, t["b_ada"][l].rearrange("(r p) -> r p", p=P)),
                    (0, V_GATTN, t["g_attn"][l].rearrange("(r p) -> r p", p=P)),
                    (0, V_GMLP, t["g_mlp"][l].rearrange("(r p) -> r p", p=P)),
                    (1, V_TAP, t["conv_w"][l].rearrange("k (r p) -> (k r) p", p=P)),
                    (1, V_CONVB, t["conv_b"][l].rearrange("(r p) -> r p", p=P)),
                    (2, V_LNG, t["conv_ln_g"][l].rearrange("(r p) -> r p", p=P)),
                    (2, V_LNB, t["conv_ln_b"][l].rearrange("(r p) -> r p", p=P)),
                    (2, V_QN, t["q_norm_g"][l:l + 1]),
                    (2, V_KN, t["k_norm_g"][l:l + 1]),
                    (2, V_GF, t["g_final"].rearrange("(r p) -> r p", p=P)),
                ):
                    sp.dma_start(vrows[r:r + src.shape[0], l, b, :], src).then_inc(vecs_in, 16)

            for l in range(DEPTH):
                w_of = {"in1": t["w_in"][l], "in2": t["w_in"][l], "out": t["w_out"][l],
                        "up": t["w_mlp1"][l], "down": t["w_mlp2"][l]}

                def load_pair(kind, n, i, c, a, last, w_of=w_of):
                    first_col = {"in2": i + IN1, "up": i + UP * c}.get(kind, i) * 512
                    first_row = c * D if kind == "down" else 0
                    for s in range(4):
                        after(sp, lo_ready, 8 * n + 2 * s - 6)
                        src = w_of[kind][bass.ds(first_row + (s % 2) * (D // 2), D // 2),
                                         bass.ds(first_col + (s // 2) * 256, 256)]
                        sp.dma_start(raw[:, s, :, :],
                                     src.rearrange("(k p) n -> p k n", p=P)).then_inc(raw_landed[s], 16)

                walk(sp, l, load_pair, lambda name, c: None)
            for b in range(8):
                s, q = b % 2, b // 2
                sp.wait_ge(out_drained, b + 1)
                sp.dma_start(t["y"][s].rearrange("a q d -> (a q) d")[:, q * 512:(q + 1) * 512],
                             xtok[:, s, q * 512:(q + 1) * 512]).then_inc(y_stored, 16)
            sp.wait_ge(y_stored, 8 * 16)
            sp.wait_ge(kv_stored, DEPTH * 4 * 16)

        @block.gpsimd
        def _(pool):
            def job(l, b):
                for s in range(4):
                    after(pool, ada_used, 4 * (l * BANKS + b) + s - 1)
                    src = t["w_ada"][l].rearrange("(p k) n -> p k n", k=KT)
                    pool.dma_start(ada[:, s % 2, :, :],
                                   src[:, 4 * s:4 * s + 4, bass.ds(b * 512, 512)]).then_inc(ada_landed[s % 2], 16)

            job(0, 0)
            with pool.Fori(1, BANKS) as b:
                job(0, b)
            with pool.Fori(0, BANKS) as b:
                job(1, b)

        @block.tensor
        def _(pe):
            def ada_unit(a, s):
                if s == 0:
                    after(pe, rows_ready, a)
                pe.wait_ge(ada_landed[s % 2], 16 * (2 * a + s // 2 + 1))
                for q in range(4):
                    mm = pe.matmul(ada_ps[32 * q:32 * q + 32, :], cT[:, 4 * s + q, :], ada[:, s % 2, q, :],
                                   start=(s == 0), stop=(s == 3))
                mm.then_inc(ada_used, 1)

            def ada_turn(a):
                pe.wait_ge(rows_ready, a + 1)
                after(pe, mods_done, a)
                for q in range(4):
                    mm = pe.matmul(mod_ps[:, 2 * q:2 * q + 2], rows[:, q * P:(q + 1) * P], sel,
                                   start=True, stop=True)
                mm.then_inc(modps_ready, 1)

            pe.wait_ge(c_ready, 3)
            pe.wait_ge(consts_in, 16)
            for s in range(4):
                ada_unit(0, s)
            ada_turn(0)
            pe.wait_ge(vecs_in, 16 * 10 * DEPTH)
            for l in range(DEPTH):
                for b, r in ((0, P), (1, P), (2, MISC)):
                    mm = pe.transpose(pb[6 + l][:, b * P:b * P + r], vrows[0:r, l, b, :], ident[0:r, 0:r])
                mm.then_inc(vecs_turned, 1)
            pe.wait_ge(x_in, 16 * S)
            for b in range(8):
                s, q = b % 2, b // 2
                after(pe, x_ready, b - 3)
                for k in range(4):
                    mm = pe.transpose(pb[b % 4][:, k * P:(k + 1) * P],
                                      xtok[:, s, (4 * q + k) * P:(4 * q + k + 1) * P], ident)
                mm.then_inc(x_turned, 1)
            with pe.Fori(1, PRE_JOBS) as a:
                for s in range(4):
                    ada_unit(a, s)
                ada_turn(a)

            for l in range(DEPTH):
                def pair(kind, n, i, c, a, last, l=l):
                    acts = act2 if kind in ("out", "down") else hs
                    for g in range(2):
                        after(pe, bank_freed, 4 * n + 2 * g - 2)
                        for h in range(4):
                            pe.wait_ge(lo_ready, 8 * n + 4 * g + h + 1)
                            if kind == "down":
                                pe.wait_ge(act2_ready, hidden_base(l, c) + 4 * (h + 1))
                            elif kind != "out":
                                pe.wait_ge(hs_ready, (2 * l + (kind == "up")) * NORM_STEPS + 8 * (h + 1))
                            for k in range(4):
                                for j in range(2):
                                    k_ = 4 * h + k
                                    bank = pb[2 * g + j]
                                    pe.matmul(bank[:, :], hi[:, h, k, j * P:(j + 1) * P], acts[:, k_, :],
                                              start=(k_ == 0), stop=False)
                                    mm = pe.matmul(bank[:, TOK:2 * TOK], lo[:, h, k, j * P:(j + 1) * P],
                                                   acts[:, k_, 0:TOK], start=False, stop=(k_ == KT - 1))
                            mm.then_inc(half_used, 1)
                            if a is not None and h % 2 == 0:
                                ada_unit(a, 2 * g + h // 2)
                    if a is not None:
                        ada_turn(a)

                def column_sums(bank, tiles):
                    for k, tile in enumerate(tiles):
                        mm = pe.matmul(bank, ones[:, :], tile, start=(k == 0), stop=(k == len(tiles) - 1))
                    return mm

                def attention(l=l):
                    a = l * BANKS + (15 if l == 0 else 19)
                    pe.wait_ge(bank_freed, 4 * (l * PAIRS_LAYER + IN1 + IN2))
                    for r, z in enumerate((QW, QW + 4)):
                        pe.matmul(pb[r][:, :], perm, zq[:, z:z + 4, P:TOK], start=True, stop=True)\
                          .then_inc(swap_ready, 1)
                    for s, bank in enumerate((7, 3)):
                        for v, z in enumerate((VG, VG + 1, VW, VW + 1)):
                            mm = pe.transpose(pb[bank][:, v * P:(v + 1) * P], zq[:, z, s * P:(s + 1) * P], ident)
                        mm.then_inc(turn_ready, 1)
                    pe.wait_ge(cache_landed, 64 * (l + 1))
                    for v in range(2 * KV):
                        mm = pe.transpose(pb[6][:, v * P:(v + 1) * P], ktokc[:, v, :], ident)
                    mm.then_inc(turn_ready, 1)
                    pe.wait_ge(conv_tap, TAP_OPS * (l + 1))
                    column_sums(pb[2][:, 0:TOK], [yconv[:, ch, :] for ch in range(CT)]).then_inc(conv_pe, 1)
                    for q, bank in enumerate((0, 1, 3, 7)):
                        pe.wait_ge(qsq_ready, 2 * l + q // 2 + 1)
                        if bank < 2:
                            pe.wait_ge(rope_done, 4 * l + bank + 1)
                        else:
                            pe.wait_ge(turn_drained, 4 * l + (2 if bank == 3 else 1))
                        column_sums(pb[bank][:, :], [qsq[:, 2 * q:2 * q + 2, :]]).then_inc(qstat_ready, 1)
                    pe.wait_ge(conv_act, 5 * l + 2)
                    column_sums(pb[2][:, 0:TOK], [ysq[:, ch, :] for ch in range(CT)]).then_inc(conv_pe, 1)
                    for s in range(4):
                        ada_unit(a, s)
                    pe.wait_ge(qnorm_done, 2 * (l + 1))
                    for r, (z, bank) in enumerate(((QG, 6), (QG + 4, 0))):
                        if bank == 6:
                            pe.wait_ge(turn_drained, 4 * l + 3)
                        else:
                            pe.wait_ge(qstd_ready, 4 * l + 1)
                        pe.matmul(pb[bank][:, :], perm, zq[:, z:z + 4, P:TOK], start=True, stop=True)\
                          .then_inc(swap_ready, 1)
                    pe.wait_ge(qstd_ready, 4 * l + 3)
                    for v, z in enumerate((KG, KG + 1, KW, KW + 1)):
                        mm = pe.transpose(pb[3][:, v * P:(v + 1) * P], zq[:, z, 0:P], ident)
                    mm.then_inc(turn_ready, 1)
                    ada_turn(a)

                    pe.wait_ge(rope_done, 4 * (l + 1))
                    pe.wait_ge(turn_drained, 4 * (l + 1))
                    pe.wait_ge(qstd_ready, 4 * (l + 1))
                    pe.wait_ge(conv_act, 5 * l + 3)
                    for it in range(2 * HEADS + 3):
                        if it < 2 * HEADS:
                            scores(l, it)
                        if 0 <= it - 2 < 2 * HEADS:
                            turn_probs(l, it - 2)
                        if 0 <= it - 3:
                            values(l, it - 3)

                def scores(l, e):
                    win, h, q, k, v = head(e)
                    if e >= 2:
                        pe.wait_ge(exp_ready, exps_before(l, e - 1))
                    bank = pb[2 if e % 2 == 0 else 6]
                    pe.matmul(bank[:, 0:P], zq[:, q, 0:P], zq[:, k, 0:P], start=True, stop=True)
                    pe.matmul(bank[:, P:2 * P], zq[:, q, P:TOK], kcT[:, v, :], start=True, stop=True)
                    pe.matmul(bank[:, 2 * P:3 * P], zq[:, q, P:TOK], zq[:, k, P:TOK], start=True, stop=True)\
                      .then_inc(score_ready, 1)

                def turn_probs(l, e):
                    base = 2 * HEADS * l
                    pe.wait_ge(prob_ready, 2 * (base + e + 1))
                    if e >= 2:
                        pe.wait_ge(probT_ready, base + e - 1)
                    bank = pb[7 if e % 2 == 0 else 3]
                    for b in range(3):
                        mm = pe.transpose(bank[:, b * P:(b + 1) * P], prob[:, e % 4, b * P:(b + 1) * P], ident)
                    mm.then_inc(probT_ps, 1)

                def values(l, e):
                    win, h, q, k, v = head(e)
                    pe.wait_ge(probT_ready, 2 * HEADS * l + e + 1)
                    if e >= 2:
                        pe.wait_ge(act2_ready, l * ACT2_LAYER + 1 + e - 1)
                    bank = pb[e % 2]
                    pe.matmul(bank[:, 0:P], vtok[:, 0, v, :], probT[:, e % 2, 0:P], start=True, stop=True)
                    pe.matmul(bank[:, P:TOK], vc[:, v, :], probT[:, e % 2, P:2 * P], start=True, stop=False)
                    pe.matmul(bank[:, P:TOK], vtok[:, 1, v, :], probT[:, e % 2, 2 * P:3 * P],
                              start=False, stop=True).then_inc(out_ready, 1)

                def stage(name, c, l=l):
                    if name in ("norm1", "norm2"):
                        if name == "norm1" and l == 0:
                            pe.wait_ge(ssq_set, 1)
                        else:
                            pe.wait_ge(ssq_steps, ssq_base(l, 0) if name == "norm2" else ssq_base(l, -1))
                        column_sums(pb[7][:, 0:TOK], [ssq[:, :]]).then_inc(stat_ready, 1)
                    elif name == "attention":
                        attention()
                        pe.wait_ge(act2_ready, l * ACT2_LAYER + MIX_STEPS)

                walk(pe, l, pair, stage)

            pe.wait_ge(ssq_steps, ssq_base(DEPTH, -1))
            pe.matmul(pb[7][:, 0:TOK], ones[:, :], ssq[:, :], start=True, stop=True).then_inc(stat_ready, 1)
            for b in range(8):
                s, q = b % 2, b // 2
                pe.wait_ge(yT_ready, 8 * (q + 1))
                after(pe, out_drained, b - 3)
                for k in range(4):
                    mm = pe.transpose(pb[b % 4][:, k * P:(k + 1) * P], yT[:, 4 * q + k, s * P:(s + 1) * P], ident)
                mm.then_inc(out_turned, 1)

        @block.scalar
        def _(act):
            def split_hi(n, o):
                act.wait_ge(raw_landed[(o // 2) % 4], 16 * (n + o // 8 + 1))
                after(act, half_used, 8 * n + o - 3)
                act.activation(hi[:, o % 4, :, :], raw[:, (o // 2) % 4, 4 * (o % 2):4 * (o % 2) + 4, :],
                               ACT.Copy).then_inc(hi_ready, 1)

            def ada_rows(a):
                act.wait_ge(ada_used, 4 * a + 4)
                after(act, modps_ready, a)
                act.activation(rows[:, :], ada_ps[:, :], ACT.Copy).then_inc(rows_ready, 1)

            act.wait_ge(c_in, 32)
            act.activation(csig[:, :, :], craw[:, :, :], ACT.Sigmoid).then_inc(c_sig, 1)
            ada_rows(0)
            for l in range(DEPTH):
                act.wait_ge(vecs_turned, l + 1)
                flat = vecs[:, l, :, :].rearrange("p b r -> p (b r)")
                act.activation(flat[:, 0:2 * P + MISC], pb[6 + l][:, 0:2 * P + MISC], ACT.Copy)\
                   .then_inc(vecs_ready, 1)
            for b in range(8):
                s, q = b % 2, b // 2
                act.wait_ge(x_turned, b + 1)
                act.activation(xT[:, 4 * q:4 * q + 4, s * P:(s + 1) * P],
                               pb[b % 4][:, :].rearrange("p (k q) -> p k q", k=4), ACT.Copy).then_inc(x_ready, 1)
            act.wait_ge(x_ready, 8)
            act.activation(xsq[:, :, :], xT[:, :, :], ACT.Square).then_inc(xsq_ready, 1)
            with act.Fori(1, PRE_JOBS) as a:
                ada_rows(a)
            for o in range(3):
                act.wait_ge(raw_landed[o // 2], 16)
                act.activation(hi[:, o, :, :], raw[:, o // 2, 4 * (o % 2):4 * (o % 2) + 4, :], ACT.Copy)\
                   .then_inc(hi_ready, 1)

            for l in range(DEPTH):
                def pair(kind, n, i, c, a, last, l=l):
                    for g in range(2):
                        for o in range(4 * g + 3, 4 * g + 7):
                            if not (last and o >= 8):
                                split_hi(n, o)
                        if a is not None and g == 1:
                            ada_rows(a)
                        act.wait_ge(half_used, 8 * n + 4 * g + 4)
                        for j in range(2):
                            after(act, bank_freed, 4 * n + 2 * g + j - 1)
                            act.activation(tmp[:, j, :], pb[2 * g + j][:, TOK:2 * TOK], ACT.Copy)\
                               .then_inc(tmp_ready, 1)
                        for j in range(2):
                            if kind == "up":
                                act.wait_ge(relu2_ready, up_tiles(l, c) + 4 * i + 2 * g + j + 1)
                                act.activation(act2[:, bass.ds(4 * i + 2 * g + j, 1), 0:TOK],
                                               thid[:, j:j + 1, :], ACT.Copy).then_inc(hid_hi, 1)
                            elif kind in ("out", "down"):
                                r = res_tiles(l, c) + 4 * i + 2 * g + j
                                act.wait_ge(x_updated, 2 * r + 2)
                                act.wait_ge(ssq_steps, ssq_base(l, c) + 4 * i + 2 * g + j)
                                act.activation(thid[:, j:j + 1, :], xT[:, bass.ds(4 * i + 2 * g + j, 1), :],
                                               ACT.Square).then_inc(sq_ready, 1)

                def attention(l=l):
                    for dst, src in ((ktokc[:, 0:KV, :], t["cache_glob_k"]), (ktokc[:, KV:2 * KV, :], t["cache_win_k"]),
                                     (vc[:, 0:KV, :], t["cache_glob_v"]), (vc[:, KV:2 * KV, :], t["cache_win_v"])):
                        act.dma_start(dst, src[0, l]).then_inc(cache_landed, 16)
                    act.wait_ge(bank_freed, 4 * (l * PAIRS_LAYER + IN1 + IN2))
                    for q in range(2):
                        act.activation(qsq[:, 4 * q:4 * q + 4, :], zq[:, QG + 4 * q:QG + 4 * q + 4, :], ACT.Square)\
                           .then_inc(qsq_ready, 1)
                    for s, bank in enumerate((7, 3)):
                        act.wait_ge(turn_ready, 4 * l + s + 1)
                        act.activation(vtok[:, s, :, :], pb[bank][:, :].rearrange("p (v d) -> p v d", v=4), ACT.Copy)\
                           .then_inc(turn_drained, 1)
                    act.wait_ge(turn_ready, 4 * l + 3)
                    act.activation(kcT[:, :, :], pb[6][:, :].rearrange("p (v d) -> p v d", v=4), ACT.Copy)\
                       .then_inc(turn_drained, 1)
                    act.wait_ge(turn_drained, 4 * l + 1)
                    act.dma_start(t["new_glob_v"][0, l], vtok[:, 0, 0:KV, :]).then_inc(kv_stored, 16)
                    act.dma_start(t["new_win_v"][0, l], vtok[:, 0, KV:2 * KV, :]).then_inc(kv_stored, 16)
                    act.wait_ge(conv_pe, 2 * l + 1)
                    act.activation(nmean[:, :], pb[2][:, 0:TOK], ACT.Copy, scale=-1.0 / CONV).then_inc(conv_act, 1)
                    for q, bank in enumerate((0, 1, 3, 7)):
                        act.wait_ge(qstat_ready, 4 * l + q + 1)
                        act.activation(qrs[:, q, :], pb[bank][:, :], ACT.Sqrt, bias=eps[:, :], scale=1.0 / P)\
                           .then_inc(qstd_ready, 1)
                    act.wait_ge(conv_dve, 6 * l + 1)
                    act.activation(ysq[:, :, :], yconv[:, :, :], ACT.Square).then_inc(conv_act, 1)
                    act.wait_ge(conv_pe, 2 * l + 2)
                    act.activation(std[:, :], pb[2][:, 0:TOK], ACT.Sqrt, bias=eps[:, :], scale=1.0 / CONV)\
                       .then_inc(conv_act, 1)
                    act.wait_ge(turn_ready, 4 * l + 4)
                    act.activation(ktok[:, :, :], pb[3][:, :].rearrange("p (v d) -> p v d", v=4), ACT.Copy)\
                       .then_inc(turn_drained, 1)
                    act.wait_ge(conv_dve, 6 * l + 5)
                    act.activation(ysq[:, :, :], yconv[:, :, :], ACT.Sigmoid).then_inc(conv_act, 1)
                    act.wait_ge(turn_drained, 4 * l + 4)
                    act.dma_start(t["new_glob_k"][0, l], ktok[:, 0:KV, :]).then_inc(kv_stored, 16)
                    act.dma_start(t["new_win_k"][0, l], ktok[:, KV:2 * KV, :]).then_inc(kv_stored, 16)
                    ada_rows(l * BANKS + (15 if l == 0 else 19))
                    act.wait_ge(conv_dve, 6 * l + 6)
                    act.activation(act2[:, 0:CT, 0:TOK], yconv[:, :, :], ACT.Copy).then_inc(conv_act, 1)
                    for it in range(2 * HEADS + 3):
                        if it < 2 * HEADS:
                            exps(l, it)
                        if 0 <= it - 2 < 2 * HEADS:
                            drain_probs(l, it - 2)
                        if 0 <= it - 3:
                            head_hi(l, it - 3)
                    act.wait_ge(kv_stored, 64 * (l + 1))

                def exps(l, e):
                    win, h, q, k, v = head(e)
                    base = 2 * HEADS * l
                    bank = pb[2 if e % 2 == 0 else 6]
                    act.wait_ge(max_ready, base + e + 1)
                    if e >= 4:
                        act.wait_ge(probT_ps, base + e - 3)
                    for s, (x, y) in enumerate(((0, P), (P, 3 * P))):
                        act.activation(prob[:, e % 4, x:y], bank[:, x:y], ACT.Exp, bias=nb[:, e, s:s + 1],
                                       scale=SCALE, accum_out=rsum[:, e, s:s + 1]).then_inc(exp_ready, 1)
                    if win:
                        act.activation(esink[:, e, :], nb[:, e, :], ACT.Exp, bias=sinks[:, l, h:h + 1])\
                           .then_inc(exp_ready, 1)

                def drain_probs(l, e):
                    base = 2 * HEADS * l
                    act.wait_ge(probT_ps, base + e + 1)
                    if e >= 2:
                        act.wait_ge(out_ready, base + e - 1)
                    act.activation(probT[:, e % 2, :], pb[7 if e % 2 == 0 else 3][:, 0:3 * P], ACT.Copy)\
                       .then_inc(probT_ready, 1)

                def head_hi(l, e):
                    win, h, q, k, v = head(e)
                    act.wait_ge(out_ready, 2 * HEADS * l + e + 1)
                    act.activation(act2[:, mix_tile(e), 0:TOK], pb[e % 2][:, 0:TOK], ACT.Copy).then_inc(out_hi, 1)

                def norm(q, shift, l=l):
                    act.wait_ge(stat_ready, q + 1)
                    act.activation(std[:, :], pb[7][:, 0:TOK], ACT.Sqrt, bias=eps[:, :], scale=1.0 / D)\
                       .then_inc(std_ready, 1)
                    act.wait_ge(mods_done, l * BANKS + (shift + KT) // 4)
                    with act.Fori(0, KT // UNROLL_K) as i:
                        for k in range(UNROLL_K):
                            for s in range(S):
                                act.wait_ge(norm_y, q * NORM_STEPS + 4 * i + 2 * k + s + 1)
                                act.activation(hs[:, bass.ds(UNROLL_K * i + k, 1), s * P:(s + 1) * P],
                                               ybuf[:, 2 * k + s:2 * k + s + 1, :], ACT.Identity,
                                               bias=mods[:, l, bass.ds(shift + UNROLL_K * i + k, 1), s])\
                                   .then_inc(norm_hi, 1)

                def stage(name, c, l=l):
                    if name == "norm1":
                        norm(2 * l, SHIFT1)
                    elif name == "norm2":
                        norm(2 * l + 1, SHIFT2)
                    elif name == "gate":
                        act.wait_ge(bank_freed, 4 * (l * PAIRS_LAYER + IN1))
                        act.activation(zc[:, CT:2 * CT, :], zc[:, CT:2 * CT, :], ACT.Sigmoid)\
                           .then_inc(gate_sig, 1)
                    elif name == "attention":
                        attention()

                walk(act, l, pair, stage)

            act.wait_ge(stat_ready, 2 * DEPTH + 1)
            act.activation(std[:, :], pb[7][:, 0:TOK], ACT.Sqrt, bias=eps[:, :], scale=1.0 / D).then_inc(std_ready, 1)
            for b in range(8):
                s, q = b % 2, b // 2
                act.wait_ge(out_turned, b + 1)
                act.activation(xtok[:, s, q * 512:(q + 1) * 512], pb[b % 4][:, :], ACT.Copy).then_inc(out_drained, 1)

        @block.vector
        def _(dve):
            def split_lo(n, o):
                dve.wait_ge(hi_ready, 8 * n + o + 1)
                dve.tensor_tensor(lo[:, o % 4, :, :], raw[:, (o // 2) % 4, 4 * (o % 2):4 * (o % 2) + 4, :],
                                  hi[:, o % 4, :, :].bitcast(f32), ALU.subtract).then_inc(lo_ready, 1)

            def add_bias(a, l, b):
                dve.wait_ge(modps_ready, a + 1)
                tiles = bass.ds(4 * b, 4)
                dve.tensor_tensor(mods[:, l, tiles, :], mod_ps[:, 0:8].rearrange("p (k s) -> p k s", s=S),
                                  vecs[:, l, 0, tiles].unsqueeze(2).to_broadcast([P, 4, S]), ALU.add)\
                   .then_inc(mods_done, 1)

            own = Steps(dve, dve_step)
            dve.memset(cT[:, :, :], 0.0).then_inc(c_ready, 1)
            dve.memset(ones[:, :], 1.0).then_inc(ones_set, 1)
            dve.memset(eps[:, :], EPS).then_inc(ones_set, 1)
            dve.wait_ge(c_sig, 1)
            dve.wait_ge(c_ready, 1)
            for s in range(S):
                dve.tensor_tensor(cT[:, :, s:s + 1], craw[:, s, :].unsqueeze(2), csig[:, s, :].unsqueeze(2),
                                  ALU.mult).then_inc(c_ready, 1)
            dve.wait_ge(sinks_in, 16)
            own.done(dve.tensor_scalar(nsinks[:, :, :], sinks[:, :, :], -1.0, None, ALU.mult))
            dve.wait_ge(vecs_ready, 1)
            add_bias(0, 0, 0)
            dve.wait_ge(xsq_ready, 1)
            dve.tensor_reduce(ssq[:, :], xsq[:, :, :].rearrange("p k q -> p q k"), AX.X, ALU.add).then_inc(ssq_set, 1)
            with dve.Fori(1, PRE_JOBS) as a:
                add_bias(a, 0, a)
            for o in range(3):
                dve.wait_ge(hi_ready, o + 1)
                dve.tensor_tensor(lo[:, o, :, :], raw[:, o // 2, 4 * (o % 2):4 * (o % 2) + 4, :],
                                  hi[:, o, :, :].bitcast(f32), ALU.subtract).then_inc(lo_ready, 1)
            dve.wait_ge(vecs_ready, DEPTH)

            for l in range(DEPTH):
                def pair(kind, n, i, c, a, last, l=l):
                    for g in range(2):
                        for o in range(4 * g + 3, 4 * g + 7):
                            if not (last and o >= 8):
                                split_lo(n, o)
                        for j in range(2):
                            tile = bass.ds(4 * i + 2 * g + j, 1)
                            done = 4 * n + 2 * g + j + 1
                            bank = pb[2 * g + j][:, 0:TOK]
                            dve.wait_ge(tmp_ready, done)
                            if kind in ("in1", "in2"):
                                z = zc if kind == "in1" else zq
                                dve.tensor_tensor(z[:, tile, :], bank.unsqueeze(1), tmp[:, j:j + 1, :], ALU.add)\
                                   .then_inc(bank_freed, 1)
                                continue
                            dve.tensor_tensor(tsum[:, j, :], bank, tmp[:, j, :], ALU.add).then_inc(bank_freed, 1)
                            dve.wait_ge(bank_freed, done)
                            if kind == "up":
                                dve.scalar_tensor_tensor(thid[:, j, :], tsum[:, j, :], 0.0, tsum[:, j, :],
                                                         ALU.max, ALU.mult).then_inc(relu2_ready, 1)
                            else:
                                gate = GATE1 if kind == "out" else GATE2
                                for s in range(S):
                                    x = xT[:, tile, s * P:(s + 1) * P]
                                    dve.scalar_tensor_tensor(
                                        x, tsum[:, j:j + 1, s * P:(s + 1) * P],
                                        mods[:, l, bass.ds(gate + 4 * i + 2 * g + j, 1), s], x,
                                        ALU.mult, ALU.add).then_inc(x_updated, 1)
                        for j in range(2):
                            if kind == "up":
                                tile = bass.ds(4 * i + 2 * g + j, 1)
                                dve.wait_ge(hid_hi, up_tiles(l, c) + 4 * i + 2 * g + j + 1)
                                dve.tensor_tensor(act2[:, tile, TOK:2 * TOK], thid[:, j:j + 1, :],
                                                  act2[:, tile, 0:TOK].bitcast(f32), ALU.subtract)\
                                   .then_inc(act2_ready, 1)
                            elif kind in ("out", "down"):
                                r = res_tiles(l, c) + 4 * i + 2 * g + j
                                dve.wait_ge(sq_ready, r + 1)
                                dve.wait_ge(ssq_steps, ssq_base(l, c) + 4 * i + 2 * g + j + 1)
                                dve.tensor_tensor(ssq[:, :], ssq[:, :], thid[:, j, :], ALU.add)\
                                   .then_inc(ssq_steps, 1)
                        if kind == "in2":
                            for tap in range(TAPS_PAIR // 2):
                                conv_tap_ops(l, TAPS_PAIR * i + g * (TAPS_PAIR // 2) + tap + 1)
                    if a is not None:
                        b = a - l * BANKS
                        if kind == "up" and not isinstance(c, int):
                            add_bias(a, l + 1, b - BANKS)
                        else:
                            add_bias(a, l, b)

                def conv_tap_ops(l, tap):
                    for ch in range(CT):
                        dve.wait_ge(conv_tap, TAP_OPS * l + 4 * (tap - 1) + ch + 1)
                        y = yconv[:, ch, :].rearrange("p (s q) -> p s q", s=S)
                        dve.scalar_tensor_tensor(y, hpad[:, ch, :, bass.ds(tap, P)],
                                                 vecs[:, l, 1, bass.ds(4 * tap + ch, 1)], y,
                                                 ALU.mult, ALU.add).then_inc(conv_tap, 1)

                def gate(l=l):
                    own.done(dve.memset(hpad[:, :, :, 0:HALO].rearrange("p c s q -> p (c s) q"), 0.0))
                    own.done(dve.memset(hpad[:, :, :, HALO + P:2 * HALO + P].rearrange("p c s q -> p (c s) q"), 0.0))
                    dve.wait_ge(gate_sig, l + 1)
                    g = zc[:, CT:2 * CT, :]
                    own.link(dve.tensor_tensor(
                        hpad[:, :, :, HALO:HALO + P].rearrange("p c s q -> p (c s) q"),
                        zc[:, 0:CT, :].rearrange("p c (s q) -> p (c s) q", s=S),
                        g.rearrange("p c (s q) -> p (c s) q", s=S), ALU.mult))
                    for ch in range(CT):
                        dve.tensor_scalar(yconv[:, ch, :].rearrange("p (s q) -> p s q", s=S),
                                          hpad[:, ch, :, 0:P], vecs[:, l, 1, ch:ch + 1],
                                          vecs[:, l, 1, V_CONVB + ch:V_CONVB + ch + 1], ALU.mult, ALU.add)\
                           .then_inc(conv_tap, 1)

                def rope(r, z, bank, l=l):
                    def rows4(ap):
                        return ap.unsqueeze(1).to_broadcast([P, 4, P])
                    x = zq[:, z:z + 4, P:TOK]
                    rt = rot[:, r % 2, :].rearrange("p (h q) -> p h q", h=4)
                    dve.wait_ge(swap_ready, 4 * l + r + 1)
                    own.done(dve.tensor_tensor(rt, pb[bank][:, :].rearrange("p (h q) -> p h q", h=4),
                                               rows4(sinT), ALU.mult))
                    own.link(dve.tensor_tensor(x, x, rows4(cosT), ALU.mult))
                    dve.tensor_tensor(x, x, rt, ALU.add).then_inc(rope_done, 1)

                def attention(l=l):
                    rope(0, QW, 0)
                    rope(1, QW + 4, 1)
                    dve.wait_ge(conv_act, 5 * l + 1)
                    dve.tensor_tensor(yconv[:, :, :], yconv[:, :, :],
                                      nmean[:, :].unsqueeze(1).to_broadcast([P, CT, TOK]), ALU.add)\
                       .then_inc(conv_dve, 1)
                    for q in range(4):
                        dve.wait_ge(qstd_ready, 4 * l + q + 1)
                        last = own.done(dve.reciprocal(qrs[:, q, :], qrs[:, q, :]))
                    own.wait(last)
                    flat = qrs[:, :, :].rearrange("p q n -> p (q n)")
                    for z, m, col in ((QG, HEADS, V_QN), (KG, KV, V_KN)):
                        x = zq[:, z:z + m, :].rearrange("p h q -> p (h q)")
                        dve.scalar_tensor_tensor(x, x, vecs[:, l, 2, col:col + 1], flat[:, z * TOK:(z + m) * TOK],
                                                 ALU.mult, ALU.mult).then_inc(qnorm_done, 1)
                    dve.wait_ge(conv_act, 5 * l + 3)
                    own.link(dve.reciprocal(rstd[:, :], std[:, :]))
                    dve.wait_ge(conv_dve, 6 * l + 1)
                    own.link(dve.tensor_tensor(yconv[:, :, :], yconv[:, :, :],
                                               rstd[:, :].unsqueeze(1).to_broadcast([P, CT, TOK]), ALU.mult))
                    for ch in range(CT):
                        dve.tensor_scalar(yconv[:, ch, :], yconv[:, ch, :],
                                          vecs[:, l, 2, V_LNG + ch:V_LNG + ch + 1],
                                          vecs[:, l, 2, V_LNB + ch:V_LNB + ch + 1], ALU.mult, ALU.add)\
                           .then_inc(conv_dve, 1)
                    dve.wait_ge(qnorm_done, 2 * (l + 1))
                    rope(2, QG, 6)
                    rope(3, QG + 4, 0)
                    dve.wait_ge(conv_act, 5 * l + 4)
                    dve.tensor_tensor(yconv[:, :, :], yconv[:, :, :], ysq[:, :, :], ALU.mult).then_inc(conv_dve, 1)
                    b = 15 if l == 0 else 19
                    add_bias(l * BANKS + b, l, b)
                    dve.wait_ge(conv_act, 5 * l + 5)
                    dve.tensor_tensor(act2[:, 0:CT, TOK:2 * TOK], yconv[:, :, :],
                                      act2[:, 0:CT, 0:TOK].bitcast(f32), ALU.subtract).then_inc(act2_ready, 1)
                    for it in range(2 * HEADS + 3):
                        if it < 2 * HEADS:
                            maxima(l, it)
                        if 0 <= it - 1 < 2 * HEADS:
                            probabilities(l, it - 1)
                        if 0 <= it - 3:
                            head_lo(l, it - 3)
                    dve.wait_ge(kv_stored, 64 * (l + 1))

                def maxima(l, e):
                    win, h, q, k, v = head(e)
                    bank = pb[2 if e % 2 == 0 else 6]
                    dve.wait_ge(score_ready, 2 * HEADS * l + e + 1)
                    own.done(dve.tensor_reduce(mx[:, e, 0:1], bank[:, 0:P], AX.X, ALU.max))
                    own.link(dve.tensor_reduce(mx[:, e, 1:2], bank[:, P:3 * P], AX.X, ALU.max))
                    if win:
                        dve.tensor_scalar(nb[:, e, :], mx[:, e, :], -SCALE, nsinks[:, l, h:h + 1],
                                          ALU.mult, ALU.min).then_inc(max_ready, 1)
                    else:
                        dve.tensor_scalar(nb[:, e, :], mx[:, e, :], -SCALE, None, ALU.mult).then_inc(max_ready, 1)

                def probabilities(l, e):
                    win, h, q, k, v = head(e)
                    dve.wait_ge(exp_ready, exps_before(l, e + 1))
                    if win:
                        own.link(dve.tensor_tensor(rsum[:, e, :], rsum[:, e, :], esink[:, e, :], ALU.add))
                    own.link(dve.reciprocal(rinv[:, e, :], rsum[:, e, :]))
                    for s, (x, y) in enumerate(((0, P), (P, 3 * P))):
                        dve.tensor_scalar(prob[:, e % 4, x:y], prob[:, e % 4, x:y], rinv[:, e, s:s + 1], None,
                                          ALU.mult).then_inc(prob_ready, 1)

                def head_lo(l, e):
                    dve.wait_ge(out_hi, 2 * HEADS * l + e + 1)
                    dve.tensor_tensor(act2[:, mix_tile(e), TOK:2 * TOK], pb[e % 2][:, 0:TOK],
                                      act2[:, mix_tile(e), 0:TOK].bitcast(f32), ALU.subtract)\
                       .then_inc(act2_ready, 1)

                def norm(q, shift, scale, gain, l=l):
                    dve.wait_ge(mods_done, l * BANKS + (scale + KT) // 4)
                    own.done(dve.scalar_tensor_tensor(
                        amul[:, :, :], mods[:, l, scale:scale + KT, :], 1.0,
                        vecs[:, l, 0, gain:gain + KT].unsqueeze(2).to_broadcast([P, KT, S]), ALU.add, ALU.mult))
                    dve.wait_ge(std_ready, q + 1)
                    own.link(dve.reciprocal(rstd[:, :], std[:, :]))
                    with dve.Fori(0, KT // UNROLL_K) as i:
                        dve.wait_ge(hs_ready, q * NORM_STEPS + 4 * i)
                        for k in range(UNROLL_K):
                            for s in range(S):
                                tile = bass.ds(UNROLL_K * i + k, 1)
                                dve.scalar_tensor_tensor(
                                    ybuf[:, 2 * k + s:2 * k + s + 1, :], xT[:, tile, s * P:(s + 1) * P],
                                    amul[:, tile, s], rstd[:, s * P:(s + 1) * P].unsqueeze(1),
                                    ALU.mult, ALU.mult).then_inc(norm_y, 1)
                        for k in range(UNROLL_K):
                            for s in range(S):
                                tile = bass.ds(UNROLL_K * i + k, 1)
                                dve.wait_ge(norm_hi, q * NORM_STEPS + 4 * i + 2 * k + s + 1)
                                dve.scalar_tensor_tensor(
                                    hs[:, tile, TOK + s * P:TOK + (s + 1) * P], ybuf[:, 2 * k + s:2 * k + s + 1, :],
                                    mods[:, l, bass.ds(shift + UNROLL_K * i + k, 1), s],
                                    hs[:, tile, s * P:(s + 1) * P].bitcast(f32),
                                    ALU.add, ALU.subtract).then_inc(hs_ready, 1)

                def stage(name, c, l=l):
                    if name == "norm1":
                        norm(2 * l, SHIFT1, SCALE1, V_GATTN)
                    elif name == "norm2":
                        norm(2 * l + 1, SHIFT2, SCALE2, V_GMLP)
                    elif name == "gate":
                        gate()
                    elif name == "attention":
                        attention()
                    elif name == "clear":
                        dve.memset(ssq[:, :], 0.0).then_inc(ssq_steps, 1)

                walk(dve, l, pair, stage)

            dve.wait_ge(std_ready, 2 * DEPTH + 1)
            own.link(dve.reciprocal(rstd[:, :], std[:, :]))
            for k in range(KT):
                for s in range(S):
                    dve.scalar_tensor_tensor(yT[:, k, s * P:(s + 1) * P], xT[:, k, s * P:(s + 1) * P],
                                             vecs[:, 0, 2, V_GF + k:V_GF + k + 1], rstd[:, s * P:(s + 1) * P],
                                             ALU.mult, ALU.mult).then_inc(yT_ready, 1)


def head(e):
    win, h = e < HEADS, e % HEADS
    kv = h // GROUP
    return win, h, (QW if win else QG) + h, (KW if win else KG) + kv, (KV if win else 0) + kv


def mix_tile(e):
    return CT + HEADS + e if e < HEADS else CT + e - HEADS


def exps_before(l, e):
    return 5 * HEADS * l + 3 * min(e, HEADS) + 2 * max(0, e - HEADS)


def up_tiles(l, c):
    return KT * (CHUNKS * l + c)


def constants():
    out = np.zeros((P, CONSTS), np.float32)
    p = np.arange(P)
    out[:, C_ID:C_ID + P] = np.eye(P)
    out[p ^ 32, C_PERM + p] = 1.0
    n_freq = P // 4
    inv = (np.float32(10000.0) ** (-np.arange(n_freq, dtype=np.float32) / np.float32(n_freq))).astype(np.float32)
    pos = np.arange(P)
    row, col = (pos // GRID_W).astype(np.float32), (pos % GRID_W).astype(np.float32)
    ang = np.concatenate([row[:, None] * inv] * 2 + [col[:, None] * inv] * 2, axis=1).T.astype(np.float64)
    out[:, C_COS:C_COS + P] = np.cos(ang)
    out[:, C_SIN:C_SIN + P] = np.sin(ang) * np.where((p // 32) % 2 == 0, -1.0, 1.0)[:, None]
    for s in range(S):
        out[s::32, C_SEL + s] = 1.0
    return out


_INS = ["x_prompt", "x_sample", "cache_glob_k", "cache_glob_v", "cache_win_k", "cache_win_v", "c", "c_ctx",
        "w_ada", "b_ada", "g_attn", "g_mlp", "w_in", "conv_w", "conv_b", "conv_ln_g", "conv_ln_b",
        "q_norm_g", "k_norm_g", "sink", "w_out", "w_mlp1", "w_mlp2", "g_final"]
_OUTS = [("y_prompt", (1, P, D)), ("y_sample", (1, P, D))] + [
    (name, (1, DEPTH, P, KV, P)) for name in ("new_glob_k", "new_glob_v", "new_win_k", "new_win_v")]


def kernel(**inputs):
    import concourse.bacc as bacc
    from concourse.bass_utils import run_bass_kernel_spmd

    nc = bacc.Bacc("TRN2", target_bir_lowering=False, num_devices=1)
    arrays, t = {}, {}
    for name in _INS:
        a = np.ascontiguousarray(inputs[name])
        arrays[f"in_{name}"] = a
        t[name] = nc.dram_tensor(f"in_{name}", a.shape, mybir.dt.from_np(a.dtype), kind="ExternalInput").ap()
    arrays["in_consts"] = constants()
    t["consts"] = nc.dram_tensor("in_consts", (P, CONSTS), f32, kind="ExternalInput").ap()
    for name, shape in _OUTS:
        t[name] = nc.dram_tensor(f"out_{name}", shape, f32, kind="ExternalOutput").ap()
    t["y"] = (t["y_prompt"], t["y_sample"])
    build(nc, t)
    r = run_bass_kernel_spmd(nc, [arrays], core_ids=[0])
    return tuple(r.results[0][f"out_{name}"] for name, _ in _OUTS)
```

```python
import numpy as np
import concourse.bass as bass
from concourse import mybir

f32 = mybir.dt.float32
f32r = mybir.dt.float32r
ALU = mybir.AluOpType
ACT = mybir.ActivationFunctionType
AX = mybir.AxisListType

P = 128
S = 2
D = 2048
KT = D // P
TOK = S * P
DEPTH = 2
EPS = 1e-6
GRID_W = 64
CONV = 512
CT = CONV // P
TAPS = 31
HALO = TAPS // 2
HEADS = 6
KV = 2
GROUP = HEADS // KV
DFF = 4 * D
CHUNKS = DFF // D
SCALE = float(P) ** -0.5
IN1, IN2, IN3, OUT, UP, DOWN = 2, 3, 2, 4, 4, 4
PAIRS_LAYER = IN1 + IN2 + IN3 + OUT + CHUNKS * (UP + DOWN)
PAIRS = DEPTH * PAIRS_LAYER
BANKS = 6 * D // 512
MIX_STEPS = 1 + 2 * HEADS
ACT2_LAYER = MIX_STEPS + KT * CHUNKS
RES_LAYER = KT * (1 + CHUNKS)
UNROLL_K = 4

QG, KG, VG, QW, KW, VW = 0, 6, 8, 10, 16, 18
SHIFT1, SCALE1, GATE1, SHIFT2, SCALE2, GATE2 = (KT * n for n in range(6))
C_ID, C_PERM, C_COS, C_SIN, C_SEL = 0, 128, 256, 384, 512
CONSTS = 514
V_BADA, V_GATTN, V_GMLP = 0, 96, 112
V_TAP, V_CONVB = 0, 124
V_LNG, V_LNB, V_QN, V_KN, V_GF = 0, 4, 8, 9, 10
MISC = 26
AHEAD = 12
PRE_JOBS = 8
NORM_STEPS = KT * S
TAP_OPS = TAPS * CT
TAPS_PAIR = (TAPS - 1) // (IN2 + IN3)
PRE_SLOTS = 8


SCORE_BANKS = 2, 6


class Steps:

    def __init__(self, eng, sem):
        self.eng, self.sem, self.n = eng, sem, 0

    def done(self, ins):
        self.n += 1
        ins.then_inc(self.sem, 1)
        return self.n

    def wait(self, value):
        self.eng.wait_ge(self.sem, value)

    def link(self, ins):
        self.wait(self.done(ins))


def build(nc, t):
    at = [16640]

    def place(name, shape, dt, offset=None):
        size = 4 * int(np.prod(shape[1:]))
        if offset is None:
            offset = at[0]
            at[0] += (size + 31) // 32 * 32
        return nc.alloc_sbuf_tensor_at(name, list(shape), dt, offset=offset)

    xT = place("xT", [P, KT, TOK], f32)
    hs_at = at[0]
    hs = place("hs", [P, KT, 2 * TOK], f32r)
    act2_at = at[0]
    act2 = place("act2", [P, KT, 2 * TOK], f32r)
    raw = place("raw", [P, 4, 8, 256], f32)
    hi = place("hi", [P, 4, 4, 256], f32r)
    lo = place("lo", [P, 4, 4, 256], f32r)
    ada = place("ada", [P, 2, 4, 512], f32)
    zq_at = at[0]
    zq = place("zq", [P, 20, TOK], f32)
    tmp = place("tmp", [P, 2, TOK], f32)
    tsum = place("tsum", [P, 2, TOK], f32)
    thid = place("thid", [P, 2, TOK], f32)
    rows = place("rows", [P, 512], f32)
    mods = place("mods", [P, DEPTH, 96, S], f32)
    vecs = place("vecs", [P, DEPTH, 3, P], f32)
    cst = place("cst", [P, CONSTS], f32)
    ones = place("ones", [P, P], f32)
    ssq = place("ssq", [P, TOK], f32)
    std = place("std", [P, TOK], f32)
    rstd = place("rstd", [P, TOK], f32)
    cT = place("cT", [P, KT, 32], f32)
    craw = place("craw", [P, S, KT], f32)
    csig = place("csig", [P, S, KT], f32)
    amul = place("amul", [P, KT, S], f32)
    kcT = place("kcT", [P, 2 * KV, P], f32)
    warm = place("warm", [P, 1], f32)
    ybuf = place("ybuf", [P, 2 * UNROLL_K, P], f32)
    sinks = place("sinks", [P, DEPTH, HEADS], f32)
    nsinks = place("nsinks", [P, DEPTH, HEADS], f32)
    eps = place("eps", [P, 1], f32)
    mx = place("mx", [P, 2 * HEADS, S], f32)
    nb = place("nb", [P, 2 * HEADS, S], f32)
    rsum = place("rsum", [P, 2 * HEADS, S], f32)
    esink = place("esink", [P, 2 * HEADS, S], f32)
    rinv = place("rinv", [P, 2 * HEADS, S], f32)
    assert at[0] <= 229368, at[0]

    xtok = place("xtok", [P, S, D], f32, hs_at)
    vc = place("vc", [P, 2 * KV, P], f32, hs_at)
    vtok = place("vtok", [P, S, 2 * KV, P], f32, hs_at + 2048)
    ktok = place("ktok", [P, 2 * KV, P], f32, hs_at + 6144)
    prob = place("prob", [P, 4, 3 * P], f32, hs_at + 8192)
    probT = place("probT", [P, 2, 3 * P], f32, hs_at + 14336)
    rotw = place("rotw", [P, 2, 512], f32, hs_at + 17408)
    ycen = place("ycen", [P, CT, TOK], f32, hs_at + 21504)
    ysq = place("ysq", [P, CT, TOK], f32, hs_at + 25600)
    pre_a = place("pre_a", [P, 4, 4, 512], f32, act2_at)
    pre_q = place("pre_q", [P, 2, 4, 512], f32, zq_at)
    pre = [pre_a[:, n] for n in range(4)] + [pre_q[:, n] for n in range(2)] + [ada[:, n] for n in range(2)]
    vrows = place("vrows", [P, DEPTH, 3, P], f32, zq_at + 16384)
    qrs = place("qrs", [P, 4, 512], f32, act2_at)
    qsq = place("qsq", [P, 4, TOK], f32, act2_at + 8192)
    ktokc = place("ktokc", [P, 2 * KV, P], f32, act2_at + 12288)
    rot = place("rot", [P, 2, 512], f32, act2_at + 25600)
    zc = place("zc", [P, 2 * CT, TOK], f32, act2_at + 8192)
    hpad = place("hpad", [P, CT, S, P + 2 * HALO], f32, act2_at + 16384)
    yconv = place("yconv", [P, CT, TOK], f32, act2_at + 21504)
    nmean = place("nmean", [P, TOK], f32, act2_at + 29696)
    yT = place("yT", [P, KT, TOK], f32, act2_at)
    xsq = place("xsq", [P, KT, TOK], f32, hs_at + 16384)

    pb = [nc.alloc_psum_tensor(f"bank{n}", [P, 512], f32) for n in range(8)]
    ada_ps, mod_ps = pb[4], pb[5]

    ident = cst[:, C_ID:C_ID + P]
    perm = cst[:, C_PERM:C_PERM + P]
    cosT = cst[:, C_COS:C_COS + P]
    sinT = cst[:, C_SIN:C_SIN + P]
    sel = cst[:, C_SEL:C_SEL + 2]

    def sem(name):
        return nc.alloc_semaphore(name)

    consts_in, c_in, vecs_in, sinks_in, x_in = (
        sem("consts_in"), sem("c_in"), sem("vecs_in"), sem("sinks_in"), sem("x_in"))
    raw_landed = [sem(f"raw_landed{n}") for n in range(4)]
    pre_landed = [sem(f"pre_landed{n}") for n in range(PRE_SLOTS)]
    ada_landed = [sem(f"ada_landed{n}") for n in range(2)]
    hi_ready = sem("hi_ready")
    lo_ready = sem("lo_ready")
    half_used = sem("half_used")
    tmp_ready = sem("tmp_ready")
    bank_freed = sem("bank_freed")
    hs_ready = sem("hs_ready")
    act2_ready = sem("act2_ready")
    norm_y = sem("norm_y")
    norm_hi = sem("norm_hi")
    relu2_ready, hid_hi = sem("relu2_ready"), sem("hid_hi")
    x_updated, sq_ready, ssq_steps = sem("x_updated"), sem("sq_ready"), sem("ssq_steps")
    stat_ready, std_ready = sem("stat_ready"), sem("std_ready")
    ada_used, rows_ready = sem("ada_used"), sem("rows_ready")
    modps_ready, mods_done = sem("modps_ready"), sem("mods_done")
    dve_step = sem("dve_step")
    ones_set, eps_set, c_sig, c_ready = sem("ones_set"), sem("eps_set"), sem("c_sig"), sem("c_ready")
    vecs_turned, vecs_ready = sem("vecs_turned"), sem("vecs_ready")
    x_turned, x_ready, xsq_ready, ssq_set = sem("x_turned"), sem("x_ready"), sem("xsq_ready"), sem("ssq_set")
    cache_landed = [sem("cached_keys_landed"), sem("cached_values_landed")]
    kv_stored, y_stored = sem("kv_stored"), sem("y_stored")
    gate_sig, conv_tap = sem("gate_sig"), sem("conv_tap")
    conv_act, conv_dve, conv_pe = sem("conv_act"), sem("conv_dve"), sem("conv_pe")
    swap_ready, rope_done = sem("swap_ready"), sem("rope_done")
    turn_ready, turn_drained = sem("turn_ready"), sem("turn_drained")
    qsq_ready, qstat_ready, qstd_ready, qnorm_done = (
        sem("qsq_ready"), sem("qstat_ready"), sem("qstd_ready"), sem("qnorm_done"))
    score_ready, max_ready, exp_ready, prob_ready = (
        sem("score_ready"), sem("max_ready"), sem("exp_ready"), sem("prob_ready"))
    probT_ps, probT_ready, out_ready, out_hi = (
        sem("probT_ps"), sem("probT_ready"), sem("out_ready"), sem("out_hi"))
    out_turned, out_drained, yT_ready = sem("out_turned"), sem("out_drained"), sem("yT_ready")

    def walk(eng, layer, pair, stage):
        n = layer * PAIRS_LAYER
        a = layer * BANKS
        first, final = layer == 0, layer == DEPTH - 1
        a_in = a + PRE_JOBS if first else a + AHEAD
        stage("norm1", 0)
        if first:
            pair("in1", 0, 0, 0, a_in, False)
        with eng.Fori(int(first), IN1) as i:
            pair("in1", n + i, i, 0, a_in + i, False)
        stage("gate", 0)
        with eng.Fori(0, IN2) as i:
            pair("in2", n + IN1 + i, i, 0, a_in + IN1 + i, False)
        n += IN1 + IN2
        for i in range(IN3):
            pair("in3", n + i, IN2 + i, 0, a_in + IN1 + IN2 + i, False)
        stage("attention", 0)
        n += IN3
        stage("clear", -1)
        with eng.Fori(0, OUT) as i:
            pair("out", n + i, i, -1, a + 16 + i if first else None, False)
        stage("norm2", 0)
        n += OUT
        with eng.Fori(0, UP) as i:
            pair("up", n + i, i, 0, a + 20 + i, False)
        stage("clear", 0)
        with eng.Fori(0, DOWN) as i:
            pair("down", n + UP + i, i, 0, None, False)

        def chunk(c, end):
            m = n + (UP + DOWN) * c
            with eng.Fori(0, UP) as i:
                pair("up", m + i, i, c, a + 20 + 4 * c + i if first else None, False)
            stage("clear", c)
            with eng.Fori(0, DOWN - end) as i:
                pair("down", m + UP + i, i, c, None, False)
            if end:
                pair("down", m + UP + DOWN - 1, DOWN - 1, c, None, True)

        with eng.Fori(1, CHUNKS - final) as c:
            chunk(c, 0)
        if final:
            chunk(CHUNKS - 1, 1)

    def hidden_base(layer, c):
        return layer * ACT2_LAYER + MIX_STEPS + KT * c

    def res_tiles(layer, c):
        return layer * RES_LAYER + KT * (c + 1)

    def ssq_base(layer, c):
        return (layer * (1 + CHUNKS) + c + 1) * (1 + KT)

    def after(eng, semaphore, value):
        if not (isinstance(value, int) and value <= 0):
            eng.wait_ge(semaphore, value)

    block = nc.Block()
    with block:

        @block.sync
        def _(sp):
            sp.dma_start(craw[:, 0, :], t["c_ctx"].rearrange("(p t) -> p t", t=KT)).then_inc(c_in, 16)
            sp.dma_start(craw[:, 1, :], t["c"].rearrange("a (p t) -> (a p) t", t=KT)).then_inc(c_in, 16)
            sp.dma_start(cst[:, :], t["consts"]).then_inc(consts_in, 16)
            sp.dma_start(sinks[:, :, :].rearrange("p l h -> p (l h)"),
                         t["sink"].rearrange("l h -> (l h)").partition_broadcast(P)).then_inc(sinks_in, 16)
            for l in range(DEPTH):
                for b, r, src in (
                    (0, V_BADA, t["b_ada"][l].rearrange("(r p) -> r p", p=P)),
                    (0, V_GATTN, t["g_attn"][l].rearrange("(r p) -> r p", p=P)),
                    (0, V_GMLP, t["g_mlp"][l].rearrange("(r p) -> r p", p=P)),
                    (1, V_TAP, t["conv_w"][l].rearrange("k (r p) -> (k r) p", p=P)),
                    (1, V_CONVB, t["conv_b"][l].rearrange("(r p) -> r p", p=P)),
                    (2, V_LNG, t["conv_ln_g"][l].rearrange("(r p) -> r p", p=P)),
                    (2, V_LNB, t["conv_ln_b"][l].rearrange("(r p) -> r p", p=P)),
                    (2, V_QN, t["q_norm_g"][l:l + 1]),
                    (2, V_KN, t["k_norm_g"][l:l + 1]),
                    (2, V_GF, t["g_final"].rearrange("(r p) -> r p", p=P)),
                ):
                    sp.dma_start(vrows[r:r + src.shape[0], l, b, :], src).then_inc(vecs_in, 16)
            for s, name in enumerate(("x_prompt", "x_sample")):
                sp.dma_start(xtok[:, s, :], t[name].rearrange("a q d -> (a q) d")).then_inc(x_in, 16)
            sp.wait_ge(ada_used, 4 * PRE_JOBS - PRE_SLOTS - 1)

            for l in range(DEPTH):
                w_of = {"in1": t["w_in"][l], "in2": t["w_in"][l], "in3": t["w_in"][l], "out": t["w_out"][l],
                        "up": t["w_mlp1"][l], "down": t["w_mlp2"][l]}

                def load_pair(kind, n, i, c, a, last, w_of=w_of):
                    first_col = {"in2": i + IN1, "in3": i + IN1, "up": i + UP * c}.get(kind, i) * 512
                    first_row = c * D if kind == "down" else 0
                    for s in range(4):
                        after(sp, lo_ready, 8 * n + 2 * s - 6)
                        src = w_of[kind][bass.ds(first_row + (s % 2) * (D // 2), D // 2),
                                         bass.ds(first_col + (s // 2) * 256, 256)]
                        sp.dma_start(raw[:, s, :, :],
                                     src.rearrange("(k p) n -> p k n", p=P)).then_inc(raw_landed[s], 16)

                walk(sp, l, load_pair, lambda name, c: None)
            for b in range(8):
                s, q = b % 2, b // 2
                sp.wait_ge(out_drained, b + 1)
                sp.dma_start(t["y"][s].rearrange("a q d -> (a q) d")[:, q * 512:(q + 1) * 512],
                             xtok[:, s, q * 512:(q + 1) * 512]).then_inc(y_stored, 16)
            sp.wait_ge(y_stored, 8 * 16)
            sp.wait_ge(kv_stored, DEPTH * 4 * 16)

        @block.gpsimd
        def _(pool):
            def job(l, b):
                for s in range(4):
                    after(pool, ada_used, 4 * (l * BANKS + b) + s - 1)
                    src = t["w_ada"][l].rearrange("(p k) n -> p k n", k=KT)
                    pool.dma_start(ada[:, s % 2, :, :],
                                   src[:, 4 * s:4 * s + 4, bass.ds(b * 512, 512)]).then_inc(ada_landed[s % 2], 16)

            def pre_jobs(first):
                src = t["w_ada"][0].rearrange("(p k) n -> p k n", k=KT)
                for u in range(PRE_SLOTS):
                    after(pool, ada_used, 4 * first + u - PRE_SLOTS + 1)
                    pool.dma_start(pre[u], src[:, 4 * (u % 4):4 * (u % 4) + 4,
                                               bass.ds(first * 512 + (u // 4) * 512, 512)]).then_inc(pre_landed[u], 16)

            pre_jobs(0)
            with pool.Fori(1, PRE_JOBS // 2) as j:
                pre_jobs(2 * j)
            with pool.Fori(PRE_JOBS, BANKS) as b:
                job(0, b)
            with pool.Fori(0, BANKS) as b:
                job(1, b)

        @block.tensor
        def _(pe):
            def ada_unit(a, s):
                if s == 0:
                    after(pe, rows_ready, a)
                pe.wait_ge(ada_landed[s % 2], 16 * (2 * (a - PRE_JOBS) + s // 2 + 1))
                ada_products(s, ada[:, s % 2])

            def ada_products(s, unit):
                for q in range(4):
                    mm = pe.matmul(ada_ps[32 * q:32 * q + 32, :], cT[:, 4 * s + q, :], unit[:, q, :],
                                   start=(s == 0), stop=(s == 3))
                mm.then_inc(ada_used, 1)

            def pre_job(a, slot, turn):
                after(pe, rows_ready, a)
                for s in range(4):
                    pe.wait_ge(pre_landed[slot + s], 16 * turn + 16)
                    ada_products(s, pre[slot + s])

            def ada_turn(a):
                pe.wait_ge(rows_ready, a + 1)
                after(pe, mods_done, a)
                for q in range(4):
                    mm = pe.matmul(mod_ps[:, 2 * q:2 * q + 2], rows[:, q * P:(q + 1) * P], sel,
                                   start=True, stop=True)
                mm.then_inc(modps_ready, 1)

            pe.wait_ge(c_ready, 3)
            pe.wait_ge(consts_in, 16)
            pre_job(0, 0, 0)
            pe.wait_ge(vecs_in, 16 * 10 * DEPTH)
            for l in range(DEPTH):
                for b, r in ((0, P), (1, P), (2, MISC)):
                    mm = pe.transpose(pb[6 + l][:, b * P:b * P + r], vrows[0:r, l, b, :], ident[0:r, 0:r])
                mm.then_inc(vecs_turned, 1)
            ada_turn(0)
            pre_job(1, 4, 0)
            ada_turn(1)
            pe.wait_ge(x_in, 16 * S)
            for b in range(8):
                s, q = b % 2, b // 2
                after(pe, x_ready, b - 3)
                for k in range(4):
                    mm = pe.transpose(pb[b % 4][:, k * P:(k + 1) * P],
                                      xtok[:, s, (4 * q + k) * P:(4 * q + k + 1) * P], ident)
                mm.then_inc(x_turned, 1)
            with pe.Fori(1, PRE_JOBS // 2) as j:
                for m in range(2):
                    pre_job(2 * j + m, 4 * m, j)
                    ada_turn(2 * j + m)

            for l in range(DEPTH):
                def pair(kind, n, i, c, a, last, l=l):
                    acts = act2 if kind in ("out", "down") else hs
                    for g in range(2):
                        after(pe, bank_freed, 4 * n + 2 * g - 2)
                        for h in range(4):
                            pe.wait_ge(lo_ready, 8 * n + 4 * g + h + 1)
                            if kind == "down":
                                pe.wait_ge(act2_ready, hidden_base(l, c) + 4 * (h + 1))
                            elif kind != "out":
                                pe.wait_ge(hs_ready, (2 * l + (kind == "up")) * NORM_STEPS + 8 * (h + 1))
                            for k in range(4):
                                for j in range(2):
                                    k_ = 4 * h + k
                                    bank = pb[2 * g + j]
                                    pe.matmul(bank[:, :], hi[:, h, k, j * P:(j + 1) * P], acts[:, k_, :],
                                              start=(k_ == 0), stop=False)
                                    mm = pe.matmul(bank[:, TOK:2 * TOK], lo[:, h, k, j * P:(j + 1) * P],
                                                   acts[:, k_, 0:TOK], start=False, stop=(k_ == KT - 1))
                            mm.then_inc(half_used, 1)
                            if a is not None and h % 2 == 0:
                                ada_unit(a, 2 * g + h // 2)
                            if kind == "in3" and h % 2 == 1:
                                qk_norms(l, 4 * (i - IN2) + 2 * g + h // 2)
                    if a is not None:
                        ada_turn(a)

                def column_sums(bank, tiles):
                    for k, tile in enumerate(tiles):
                        mm = pe.matmul(bank, ones[:, :], tile, start=(k == 0), stop=(k == len(tiles) - 1))
                    return mm

                def qk_norms(l, step):
                    if step < 2:
                        pe.wait_ge(qsq_ready, 2 * l + step + 1)
                        for q in (2 * step, 2 * step + 1):
                            after(pe, qstd_ready, 4 * l + q - 1)
                            column_sums(pb[6 + q % 2][:, :], [qsq[:, 2 * (q % 2):2 * (q % 2) + 2, :]])\
                                .then_inc(qstat_ready, 1)
                    elif step == 2:
                        pe.wait_ge(cache_landed[0], 32 * (l + 1))
                        pe.wait_ge(qstd_ready, 4 * l + 3)
                        for v in range(2 * KV):
                            mm = pe.transpose(pb[6][:, v * P:(v + 1) * P], ktokc[:, v, :], ident)
                        mm.then_inc(turn_ready, 1)
                    elif step == 3:
                        pe.wait_ge(qnorm_done, 2 * (l + 1))
                        pe.wait_ge(qstd_ready, 4 * l + 4)
                        exchange(QG, 7)
                    elif step == 4:
                        pe.wait_ge(turn_drained, 4 * l + 1)
                        exchange(QG + 4, 6)

                def exchange(z, bank):
                    pe.matmul(pb[bank][:, :], perm, zq[:, z:z + 4, P:TOK], start=True, stop=True)\
                      .then_inc(swap_ready, 1)

                def attention(l=l):
                    a = l * BANKS + (15 if l == 0 else 19)
                    pe.wait_ge(bank_freed, 4 * (l * PAIRS_LAYER + IN1 + IN2 + IN3))
                    exchange(QW, 0)
                    exchange(QW + 4, 1)
                    for s, bank in enumerate((7, 3)):
                        if s == 0:
                            pe.wait_ge(rope_done, 4 * l + 1)
                        for v, z in enumerate((VG, VG + 1, VW, VW + 1)):
                            mm = pe.transpose(pb[bank][:, v * P:(v + 1) * P], zq[:, z, s * P:(s + 1) * P], ident)
                        mm.then_inc(turn_ready, 1)
                    pe.wait_ge(conv_tap, TAP_OPS * (l + 1))
                    pe.wait_ge(mods_done, a)
                    column_sums(pb[5][:, 0:TOK], [yconv[:, ch, :] for ch in range(CT)]).then_inc(conv_pe, 1)
                    pe.wait_ge(rope_done, 4 * l + 2)
                    for it in range(2 * HEADS + 3):
                        if it == HEADS:
                            pe.wait_ge(rope_done, 4 * (l + 1))
                        if it < 2 * HEADS:
                            scores(l, it)
                        if it == 1:
                            pe.wait_ge(conv_act, 5 * l + 2)
                            column_sums(pb[5][:, 0:TOK], [ysq[:, ch, :] for ch in range(CT)]).then_inc(conv_pe, 1)
                            pe.wait_ge(turn_drained, 4 * l + 3)
                        if it == 2:
                            pe.wait_ge(rope_done, 4 * (l + 1))
                        if 0 <= it - 2 < 2 * HEADS:
                            turn_probs(l, it - 2)
                        if 0 <= it - 3:
                            values(l, it - 3)
                        if 3 <= it < 7:
                            ada_unit(a, it - 3)
                        if it == 7:
                            pe.wait_ge(conv_act, 5 * l + 3)
                            for v, z in enumerate((KG, KG + 1, KW, KW + 1)):
                                mm = pe.transpose(pb[5][:, v * P:(v + 1) * P], zq[:, z, 0:P], ident)
                            mm.then_inc(turn_ready, 1)
                        if it == 10:
                            pe.wait_ge(turn_drained, 4 * (l + 1))
                            ada_turn(a)

                def scores(l, e):
                    win, h, q, k, v = head(e)
                    if e >= 2:
                        pe.wait_ge(exp_ready, exps_before(l, e - 1))
                    bank = pb[SCORE_BANKS[e % 2]]
                    pe.matmul(bank[:, 0:P], zq[:, q, 0:P], zq[:, k, 0:P], start=True, stop=True)
                    pe.matmul(bank[:, P:2 * P], zq[:, q, P:TOK], kcT[:, v, :], start=True, stop=True)
                    pe.matmul(bank[:, 2 * P:3 * P], zq[:, q, P:TOK], zq[:, k, P:TOK], start=True, stop=True)\
                      .then_inc(score_ready, 1)

                def turn_probs(l, e):
                    base = 2 * HEADS * l
                    pe.wait_ge(prob_ready, 2 * (base + e + 1))
                    if e >= 2:
                        pe.wait_ge(probT_ready, base + e - 1)
                    bank = pb[7 if e % 2 == 0 else 3]
                    for b in range(3):
                        mm = pe.transpose(bank[:, b * P:(b + 1) * P], prob[:, e % 4, b * P:(b + 1) * P], ident)
                    mm.then_inc(probT_ps, 1)

                def values(l, e):
                    win, h, q, k, v = head(e)
                    pe.wait_ge(probT_ready, 2 * HEADS * l + e + 1)
                    if e == 0:
                        pe.wait_ge(cache_landed[1], 32 * (l + 1))
                    if e >= 2:
                        pe.wait_ge(act2_ready, l * ACT2_LAYER + e - 1)
                    bank = pb[e % 2]
                    pe.matmul(bank[:, 0:P], vtok[:, 0, v, :], probT[:, e % 2, 0:P], start=True, stop=True)
                    pe.matmul(bank[:, P:TOK], vc[:, v, :], probT[:, e % 2, P:2 * P], start=True, stop=False)
                    pe.matmul(bank[:, P:TOK], vtok[:, 1, v, :], probT[:, e % 2, 2 * P:3 * P],
                              start=False, stop=True).then_inc(out_ready, 1)

                def stage(name, c, l=l):
                    if name in ("norm1", "norm2"):
                        if name == "norm1" and l == 0:
                            pe.wait_ge(ssq_set, 1)
                        else:
                            pe.wait_ge(ssq_steps, ssq_base(l, 0) if name == "norm2" else ssq_base(l, -1))
                        column_sums(pb[7][:, 0:TOK], [ssq[:, :]]).then_inc(stat_ready, 1)
                    elif name == "attention":
                        attention()
                        pe.wait_ge(act2_ready, l * ACT2_LAYER + MIX_STEPS)

                walk(pe, l, pair, stage)

            pe.wait_ge(ssq_steps, ssq_base(DEPTH, -1))
            pe.matmul(pb[7][:, 0:TOK], ones[:, :], ssq[:, :], start=True, stop=True).then_inc(stat_ready, 1)
            for b in range(8):
                s, q = b % 2, b // 2
                pe.wait_ge(yT_ready, 8 * (q + 1))
                after(pe, out_drained, b - 3)
                for k in range(4):
                    mm = pe.transpose(pb[b % 4][:, k * P:(k + 1) * P], yT[:, 4 * q + k, s * P:(s + 1) * P], ident)
                mm.then_inc(out_turned, 1)

        @block.scalar
        def _(act):
            def split_hi(n, o):
                act.wait_ge(raw_landed[(o // 2) % 4], 16 * (n + o // 8 + 1))
                after(act, half_used, 8 * n + o - 3)
                act.activation(hi[:, o % 4, :, :], raw[:, (o // 2) % 4, 4 * (o % 2):4 * (o % 2) + 4, :],
                               ACT.Copy).then_inc(hi_ready, 1)

            def ada_rows(a):
                act.wait_ge(ada_used, 4 * a + 4)
                after(act, modps_ready, a)
                act.activation(rows[:, :], ada_ps[:, :], ACT.Copy).then_inc(rows_ready, 1)

            act.wait_ge(c_in, 32)
            act.activation(csig[:, :, :], craw[:, :, :], ACT.Sigmoid).then_inc(c_sig, 1)
            ada_rows(0)
            for l in range(DEPTH):
                act.wait_ge(vecs_turned, l + 1)
                flat = vecs[:, l, :, :].rearrange("p b r -> p (b r)")
                act.activation(flat[:, 0:2 * P + MISC], pb[6 + l][:, 0:2 * P + MISC], ACT.Copy)\
                   .then_inc(vecs_ready, 1)
            ada_rows(1)
            for b in range(8):
                s, q = b % 2, b // 2
                act.wait_ge(x_turned, b + 1)
                act.activation(xT[:, 4 * q:4 * q + 4, s * P:(s + 1) * P],
                               pb[b % 4][:, :].rearrange("p (k q) -> p k q", k=4), ACT.Copy).then_inc(x_ready, 1)
            act.wait_ge(x_ready, 8)
            act.activation(xsq[:, :, :], xT[:, :, :], ACT.Square).then_inc(xsq_ready, 1)
            with act.Fori(2, PRE_JOBS) as a:
                ada_rows(a)
            for o in range(3):
                act.wait_ge(raw_landed[o // 2], 16)
                act.activation(hi[:, o, :, :], raw[:, o // 2, 4 * (o % 2):4 * (o % 2) + 4, :], ACT.Copy)\
                   .then_inc(hi_ready, 1)

            for l in range(DEPTH):
                def pair(kind, n, i, c, a, last, l=l):
                    for g in range(2):
                        if kind == "in3":
                            qk_norms(l, 4 * (i - IN2) + 2 * g)
                        for o in range(4 * g + 3, 4 * g + 7):
                            if not (last and o >= 8):
                                split_hi(n, o)
                        if kind == "in3":
                            qk_norms(l, 4 * (i - IN2) + 2 * g + 1)
                        if a is not None and g == 1:
                            ada_rows(a)
                        act.wait_ge(half_used, 8 * n + 4 * g + 4)
                        for j in range(2):
                            after(act, bank_freed, 4 * n + 2 * g + j - 1)
                            act.activation(tmp[:, j, :], pb[2 * g + j][:, TOK:2 * TOK], ACT.Copy)\
                               .then_inc(tmp_ready, 1)
                        for j in range(2):
                            if kind == "up":
                                act.wait_ge(relu2_ready, up_tiles(l, c) + 4 * i + 2 * g + j + 1)
                                act.activation(act2[:, bass.ds(4 * i + 2 * g + j, 1), 0:TOK],
                                               thid[:, j:j + 1, :], ACT.Copy).then_inc(hid_hi, 1)
                            elif kind in ("out", "down"):
                                r = res_tiles(l, c) + 4 * i + 2 * g + j
                                act.wait_ge(x_updated, 2 * r + 2)
                                act.wait_ge(ssq_steps, ssq_base(l, c) + 4 * i + 2 * g + j)
                                act.activation(thid[:, j:j + 1, :], xT[:, bass.ds(4 * i + 2 * g + j, 1), :],
                                               ACT.Square).then_inc(sq_ready, 1)

                def squares(l, q):
                    act.activation(qsq[:, :, :], zq[:, QG + 4 * q:QG + 4 * q + 4, :], ACT.Square)\
                       .then_inc(qsq_ready, 1)

                def deviations(l, q):
                    act.wait_ge(qstat_ready, 4 * l + q + 1)
                    act.activation(qrs[:, q, :], pb[6 + q % 2][:, :], ACT.Sqrt, bias=eps[:, :], scale=1.0 / P)\
                       .then_inc(qstd_ready, 1)

                def qk_norms(l, step):
                    if step == 0:
                        act.wait_ge(conv_tap, TAP_OPS * l + CT)
                        act.dma_start(ktokc[:, 0:KV, :], t["cache_glob_k"][0, l]).then_inc(cache_landed[0], 16)
                        act.dma_start(ktokc[:, KV:2 * KV, :], t["cache_win_k"][0, l]).then_inc(cache_landed[0], 16)
                        act.wait_ge(bank_freed, 4 * (l * PAIRS_LAYER + IN1 + IN2))
                        squares(l, 0)
                    elif step == 1:
                        deviations(l, 0)
                        deviations(l, 1)
                        squares(l, 1)
                    elif step == 2:
                        deviations(l, 2)
                        deviations(l, 3)
                    elif step == 3:
                        act.wait_ge(turn_ready, 4 * l + 1)
                        act.activation(kcT[:, :, :], pb[6][:, :].rearrange("p (v d) -> p v d", v=4), ACT.Copy)\
                           .then_inc(turn_drained, 1)

                def attention(l=l):
                    act.dma_start(vc[:, 0:KV, :], t["cache_glob_v"][0, l]).then_inc(cache_landed[1], 16)
                    act.dma_start(vc[:, KV:2 * KV, :], t["cache_win_v"][0, l]).then_inc(cache_landed[1], 16)
                    for s, bank in enumerate((7, 3)):
                        act.wait_ge(turn_ready, 4 * l + s + 2)
                        act.activation(vtok[:, s, :, :], pb[bank][:, :].rearrange("p (v d) -> p v d", v=4), ACT.Copy)\
                           .then_inc(turn_drained, 1)
                    act.wait_ge(conv_pe, 2 * l + 1)
                    act.activation(nmean[:, :], pb[5][:, 0:TOK], ACT.Copy, scale=-1.0 / CONV).then_inc(conv_act, 1)
                    act.wait_ge(turn_drained, 4 * l + 2)
                    act.dma_start(t["new_glob_v"][0, l], vtok[:, 0, 0:KV, :]).then_inc(kv_stored, 16)
                    act.dma_start(t["new_win_v"][0, l], vtok[:, 0, KV:2 * KV, :]).then_inc(kv_stored, 16)
                    act.wait_ge(conv_dve, 6 * l + 1)
                    act.activation(ysq[:, :, :], ycen[:, :, :], ACT.Square).then_inc(conv_act, 1)
                    act.wait_ge(conv_pe, 2 * l + 2)
                    act.activation(std[:, :], pb[5][:, 0:TOK], ACT.Sqrt, bias=eps[:, :], scale=1.0 / CONV)\
                       .then_inc(conv_act, 1)
                    for it in range(2 * HEADS + 3):
                        if it < 2 * HEADS:
                            exps(l, it)
                        if it == 7:
                            ada_rows(l * BANKS + (15 if l == 0 else 19))
                        if it == 8:
                            act.wait_ge(turn_ready, 4 * (l + 1))
                            act.activation(ktok[:, :, :], pb[5][:, :].rearrange("p (v d) -> p v d", v=4), ACT.Copy)\
                               .then_inc(turn_drained, 1)
                        if it == 9:
                            act.wait_ge(turn_drained, 4 * (l + 1))
                            act.dma_start(t["new_glob_k"][0, l], ktok[:, 0:KV, :]).then_inc(kv_stored, 16)
                            act.dma_start(t["new_win_k"][0, l], ktok[:, KV:2 * KV, :]).then_inc(kv_stored, 16)
                        if it == 2 * HEADS:
                            act.wait_ge(conv_dve, 6 * l + 5)
                            act.activation(ysq[:, :, :], ycen[:, :, :], ACT.Sigmoid).then_inc(conv_act, 1)
                        if 0 <= it - 3:
                            head_hi(l, it - 3)
                    act.wait_ge(conv_dve, 6 * l + 6)
                    act.activation(act2[:, 0:CT, 0:TOK], ysq[:, :, :], ACT.Copy).then_inc(conv_act, 1)
                    act.activation(warm[:, :], eps[:, :], ACT.Sqrt)
                    act.wait_ge(kv_stored, 64 * (l + 1))

                def exps(l, e):
                    win, h, q, k, v = head(e)
                    base = 2 * HEADS * l
                    bank = pb[SCORE_BANKS[e % 2]]
                    act.wait_ge(max_ready, base + e + 1)
                    if e >= 4:
                        act.wait_ge(probT_ps, base + e - 3)
                    for s, (x, y) in enumerate(((0, P), (P, 3 * P))):
                        act.activation(prob[:, e % 4, x:y], bank[:, x:y], ACT.Exp, bias=nb[:, e, s:s + 1],
                                       scale=SCALE, accum_out=rsum[:, e, s:s + 1]).then_inc(exp_ready, 1)
                    if win:
                        act.activation(esink[:, e, :], nb[:, e, :], ACT.Exp, bias=sinks[:, l, h:h + 1])\
                           .then_inc(exp_ready, 1)

                def head_hi(l, e):
                    win, h, q, k, v = head(e)
                    act.wait_ge(out_ready, 2 * HEADS * l + e + 1)
                    act.activation(act2[:, mix_tile(e), 0:TOK], pb[e % 2][:, 0:TOK], ACT.Copy).then_inc(out_hi, 1)

                def norm(q, shift, l=l):
                    act.wait_ge(stat_ready, q + 1)
                    act.activation(std[:, :], pb[7][:, 0:TOK], ACT.Sqrt, bias=eps[:, :], scale=1.0 / D)\
                       .then_inc(std_ready, 1)
                    act.wait_ge(mods_done, l * BANKS + (shift + KT) // 4)
                    with act.Fori(0, KT // UNROLL_K) as i:
                        for k in range(UNROLL_K):
                            for s in range(S):
                                act.wait_ge(norm_y, q * NORM_STEPS + S * UNROLL_K * i + 2 * k + s + 1)
                                act.activation(hs[:, bass.ds(UNROLL_K * i + k, 1), s * P:(s + 1) * P],
                                               ybuf[:, 2 * k + s:2 * k + s + 1, :], ACT.Identity,
                                               bias=mods[:, l, bass.ds(shift + UNROLL_K * i + k, 1), s])\
                                   .then_inc(norm_hi, 1)

                def stage(name, c, l=l):
                    if name == "norm1":
                        norm(2 * l, SHIFT1)
                    elif name == "norm2":
                        norm(2 * l + 1, SHIFT2)
                    elif name == "gate":
                        act.wait_ge(bank_freed, 4 * (l * PAIRS_LAYER + IN1))
                        act.activation(zc[:, CT:2 * CT, :], zc[:, CT:2 * CT, :], ACT.Sigmoid)\
                           .then_inc(gate_sig, 1)
                    elif name == "attention":
                        attention()

                walk(act, l, pair, stage)

            act.wait_ge(stat_ready, 2 * DEPTH + 1)
            act.activation(std[:, :], pb[7][:, 0:TOK], ACT.Sqrt, bias=eps[:, :], scale=1.0 / D).then_inc(std_ready, 1)
            for b in range(8):
                s, q = b % 2, b // 2
                act.wait_ge(out_turned, b + 1)
                act.activation(xtok[:, s, q * 512:(q + 1) * 512], pb[b % 4][:, :], ACT.Copy).then_inc(out_drained, 1)

        @block.vector
        def _(dve):
            def split_lo(n, o):
                dve.wait_ge(hi_ready, 8 * n + o + 1)
                dve.tensor_tensor(lo[:, o % 4, :, :], raw[:, (o // 2) % 4, 4 * (o % 2):4 * (o % 2) + 4, :],
                                  hi[:, o % 4, :, :].bitcast(f32), ALU.subtract).then_inc(lo_ready, 1)

            def add_bias(a, l, b):
                dve.wait_ge(modps_ready, a + 1)
                tiles = bass.ds(4 * b, 4)
                dve.tensor_tensor(mods[:, l, tiles, :], mod_ps[:, 0:8].rearrange("p (k s) -> p k s", s=S),
                                  vecs[:, l, 0, tiles].unsqueeze(2).to_broadcast([P, 4, S]), ALU.add)\
                   .then_inc(mods_done, 1)

            own = Steps(dve, dve_step)
            dve.memset(cT[:, :, :], 0.0).then_inc(c_ready, 1)
            dve.memset(ones[:, :], 1.0).then_inc(ones_set, 1)
            dve.memset(eps[:, :], EPS).then_inc(ones_set, 1)
            dve.wait_ge(c_sig, 1)
            dve.wait_ge(c_ready, 1)
            for s in range(S):
                dve.tensor_tensor(cT[:, :, s:s + 1], craw[:, s, :].unsqueeze(2), csig[:, s, :].unsqueeze(2),
                                  ALU.mult).then_inc(c_ready, 1)
            dve.wait_ge(sinks_in, 16)
            own.done(dve.tensor_scalar(nsinks[:, :, :], sinks[:, :, :], -1.0, None, ALU.mult))
            dve.wait_ge(vecs_ready, 1)
            add_bias(0, 0, 0)
            add_bias(1, 0, 1)
            dve.wait_ge(xsq_ready, 1)
            dve.tensor_reduce(ssq[:, :], xsq[:, :, :].rearrange("p k q -> p q k"), AX.X, ALU.add).then_inc(ssq_set, 1)
            with dve.Fori(2, PRE_JOBS) as a:
                add_bias(a, 0, a)
            for o in range(3):
                dve.wait_ge(hi_ready, o + 1)
                dve.tensor_tensor(lo[:, o, :, :], raw[:, o // 2, 4 * (o % 2):4 * (o % 2) + 4, :],
                                  hi[:, o, :, :].bitcast(f32), ALU.subtract).then_inc(lo_ready, 1)
            dve.wait_ge(vecs_ready, DEPTH)

            for l in range(DEPTH):
                def pair(kind, n, i, c, a, last, l=l):
                    for g in range(2):
                        if kind == "in3":
                            qk_norms(l, 4 * (i - IN2) + 2 * g)
                        for o in range(4 * g + 3, 4 * g + 7):
                            if not (last and o >= 8):
                                split_lo(n, o)
                        if kind == "in3":
                            qk_norms(l, 4 * (i - IN2) + 2 * g + 1)
                        for j in range(2):
                            tile = bass.ds(4 * i + 2 * g + j, 1)
                            done = 4 * n + 2 * g + j + 1
                            bank = pb[2 * g + j][:, 0:TOK]
                            dve.wait_ge(tmp_ready, done)
                            if kind in ("in1", "in2", "in3"):
                                z = zc if kind == "in1" else zq
                                dve.tensor_tensor(z[:, tile, :], bank.unsqueeze(1), tmp[:, j:j + 1, :], ALU.add)\
                                   .then_inc(bank_freed, 1)
                                continue
                            dve.tensor_tensor(tsum[:, j, :], bank, tmp[:, j, :], ALU.add).then_inc(bank_freed, 1)
                            dve.wait_ge(bank_freed, done)
                            if kind == "up":
                                dve.scalar_tensor_tensor(thid[:, j, :], tsum[:, j, :], 0.0, tsum[:, j, :],
                                                         ALU.max, ALU.mult).then_inc(relu2_ready, 1)
                            else:
                                gate = GATE1 if kind == "out" else GATE2
                                for s in range(S):
                                    x = xT[:, tile, s * P:(s + 1) * P]
                                    dve.scalar_tensor_tensor(
                                        x, tsum[:, j:j + 1, s * P:(s + 1) * P],
                                        mods[:, l, bass.ds(gate + 4 * i + 2 * g + j, 1), s], x,
                                        ALU.mult, ALU.add).then_inc(x_updated, 1)
                        for j in range(2):
                            if kind == "up":
                                tile = bass.ds(4 * i + 2 * g + j, 1)
                                dve.wait_ge(hid_hi, up_tiles(l, c) + 4 * i + 2 * g + j + 1)
                                dve.tensor_tensor(act2[:, tile, TOK:2 * TOK], thid[:, j:j + 1, :],
                                                  act2[:, tile, 0:TOK].bitcast(f32), ALU.subtract)\
                                   .then_inc(act2_ready, 1)
                            elif kind in ("out", "down"):
                                r = res_tiles(l, c) + 4 * i + 2 * g + j
                                dve.wait_ge(sq_ready, r + 1)
                                dve.wait_ge(ssq_steps, ssq_base(l, c) + 4 * i + 2 * g + j + 1)
                                dve.tensor_tensor(ssq[:, :], ssq[:, :], thid[:, j, :], ALU.add)\
                                   .then_inc(ssq_steps, 1)
                        if kind in ("in2", "in3"):
                            for tap in range(TAPS_PAIR // 2):
                                conv_tap_ops(l, TAPS_PAIR * i + g * (TAPS_PAIR // 2) + tap + 1)
                    if a is not None:
                        b = a - l * BANKS
                        if kind == "up" and not isinstance(c, int):
                            add_bias(a, l + 1, b - BANKS)
                        else:
                            add_bias(a, l, b)

                def conv_tap_ops(l, tap):
                    for ch in range(CT):
                        dve.wait_ge(conv_tap, TAP_OPS * l + 4 * (tap - 1) + ch + 1)
                        y = yconv[:, ch, :].rearrange("p (s q) -> p s q", s=S)
                        dve.scalar_tensor_tensor(y, hpad[:, ch, :, bass.ds(tap, P)],
                                                 vecs[:, l, 1, bass.ds(4 * tap + ch, 1)], y,
                                                 ALU.mult, ALU.add).then_inc(conv_tap, 1)

                def gate(l=l):
                    own.done(dve.memset(hpad[:, :, :, 0:HALO].rearrange("p c s q -> p (c s) q"), 0.0))
                    own.done(dve.memset(hpad[:, :, :, HALO + P:2 * HALO + P].rearrange("p c s q -> p (c s) q"), 0.0))
                    dve.wait_ge(gate_sig, l + 1)
                    g = zc[:, CT:2 * CT, :]
                    own.link(dve.tensor_tensor(
                        hpad[:, :, :, HALO:HALO + P].rearrange("p c s q -> p (c s) q"),
                        zc[:, 0:CT, :].rearrange("p c (s q) -> p (c s) q", s=S),
                        g.rearrange("p c (s q) -> p (c s) q", s=S), ALU.mult))
                    for ch in range(CT):
                        dve.tensor_scalar(yconv[:, ch, :].rearrange("p (s q) -> p s q", s=S),
                                          hpad[:, ch, :, 0:P], vecs[:, l, 1, ch:ch + 1],
                                          vecs[:, l, 1, V_CONVB + ch:V_CONVB + ch + 1], ALU.mult, ALU.add)\
                           .then_inc(conv_tap, 1)

                def rope(r, z, bank, place, l=l):
                    def rows4(ap):
                        return ap.unsqueeze(1).to_broadcast([P, 4, P])
                    x = zq[:, z:z + 4, P:TOK]
                    rt = place[:, r % 2, :].rearrange("p (h q) -> p h q", h=4)
                    dve.wait_ge(swap_ready, 4 * l + r + 1)
                    own.done(dve.tensor_tensor(rt, pb[bank][:, :].rearrange("p (h q) -> p h q", h=4),
                                               rows4(sinT), ALU.mult))
                    own.link(dve.tensor_tensor(x, x, rows4(cosT), ALU.mult))
                    dve.tensor_tensor(x, x, rt, ALU.add).then_inc(rope_done, 1)

                def qk_norms(l, step):
                    if step in (2, 3):
                        for q in (2 * step - 4, 2 * step - 3):
                            dve.wait_ge(qstd_ready, 4 * l + q + 1)
                            last = own.done(dve.reciprocal(qrs[:, q, :], qrs[:, q, :]))
                    if step == 3:
                        own.wait(last)
                        flat = qrs[:, :, :].rearrange("p q n -> p (q n)")
                        for z, m, col in ((QG, HEADS, V_QN), (KG, KV, V_KN)):
                            x = zq[:, z:z + m, :].rearrange("p h q -> p (h q)")
                            dve.scalar_tensor_tensor(x, x, vecs[:, l, 2, col:col + 1],
                                                     flat[:, z * TOK:(z + m) * TOK],
                                                     ALU.mult, ALU.mult).then_inc(qnorm_done, 1)
                    if step == 5:
                        dve.wait_ge(qnorm_done, 2 * (l + 1))
                        rope(0, QG, 7, rot, l)
                    if step == 6:
                        rope(1, QG + 4, 6, rot, l)

                def attention(l=l):
                    dve.wait_ge(conv_act, 5 * l + 1)
                    dve.tensor_tensor(ycen[:, :, :], yconv[:, :, :],
                                      nmean[:, :].unsqueeze(1).to_broadcast([P, CT, TOK]), ALU.add)\
                       .then_inc(conv_dve, 1)
                    for it in range(2 * HEADS + 3):
                        if it < 2 * HEADS:
                            maxima(l, it)
                        if it == 0:
                            rope(2, QW, 0, rotw, l)
                            rope(3, QW + 4, 1, rotw, l)
                        if it == 2:
                            dve.wait_ge(conv_act, 5 * l + 3)
                            own.link(dve.reciprocal(rstd[:, :], std[:, :]))
                            dve.wait_ge(conv_dve, 6 * l + 1)
                            own.link(dve.tensor_tensor(ycen[:, :, :], ycen[:, :, :],
                                                       rstd[:, :].unsqueeze(1).to_broadcast([P, CT, TOK]), ALU.mult))
                        if it == 5:
                            for ch in range(CT):
                                dve.tensor_scalar(ycen[:, ch, :], ycen[:, ch, :],
                                                  vecs[:, l, 2, V_LNG + ch:V_LNG + ch + 1],
                                                  vecs[:, l, 2, V_LNB + ch:V_LNB + ch + 1], ALU.mult, ALU.add)\
                                   .then_inc(conv_dve, 1)
                        if 0 <= it - 1 < 2 * HEADS:
                            probabilities(l, it - 1)
                        if 0 <= it - 2 < 2 * HEADS:
                            drain_probs(l, it - 2)
                        if it == 2 * HEADS + 1:
                            dve.wait_ge(conv_act, 5 * l + 4)
                            dve.tensor_tensor(ysq[:, :, :], ycen[:, :, :], ysq[:, :, :], ALU.mult)\
                               .then_inc(conv_dve, 1)
                        if 0 <= it - 3:
                            head_lo(l, it - 3)
                    b = 15 if l == 0 else 19
                    add_bias(l * BANKS + b, l, b)
                    dve.wait_ge(conv_act, 5 * l + 5)
                    dve.tensor_tensor(act2[:, 0:CT, TOK:2 * TOK], ysq[:, :, :],
                                      act2[:, 0:CT, 0:TOK].bitcast(f32), ALU.subtract).then_inc(act2_ready, 1)
                    dve.wait_ge(kv_stored, 64 * (l + 1))

                def drain_probs(l, e):
                    base = 2 * HEADS * l
                    dve.wait_ge(probT_ps, base + e + 1)
                    if e >= 2:
                        dve.wait_ge(out_ready, base + e - 1)
                    dve.tensor_copy(probT[:, e % 2, :], pb[7 if e % 2 == 0 else 3][:, 0:3 * P])\
                       .then_inc(probT_ready, 1)

                def maxima(l, e):
                    win, h, q, k, v = head(e)
                    bank = pb[SCORE_BANKS[e % 2]]
                    dve.wait_ge(score_ready, 2 * HEADS * l + e + 1)
                    own.done(dve.tensor_reduce(mx[:, e, 0:1], bank[:, 0:P], AX.X, ALU.max))
                    own.link(dve.tensor_reduce(mx[:, e, 1:2], bank[:, P:3 * P], AX.X, ALU.max))
                    if win:
                        dve.tensor_scalar(nb[:, e, :], mx[:, e, :], -SCALE, nsinks[:, l, h:h + 1],
                                          ALU.mult, ALU.min).then_inc(max_ready, 1)
                    else:
                        dve.tensor_scalar(nb[:, e, :], mx[:, e, :], -SCALE, None, ALU.mult).then_inc(max_ready, 1)

                def probabilities(l, e):
                    win, h, q, k, v = head(e)
                    dve.wait_ge(exp_ready, exps_before(l, e + 1))
                    if win:
                        own.link(dve.tensor_tensor(rsum[:, e, :], rsum[:, e, :], esink[:, e, :], ALU.add))
                    own.link(dve.reciprocal(rinv[:, e, :], rsum[:, e, :]))
                    for s, (x, y) in enumerate(((0, P), (P, 3 * P))):
                        dve.tensor_scalar(prob[:, e % 4, x:y], prob[:, e % 4, x:y], rinv[:, e, s:s + 1], None,
                                          ALU.mult).then_inc(prob_ready, 1)

                def head_lo(l, e):
                    dve.wait_ge(out_hi, 2 * HEADS * l + e + 1)
                    dve.tensor_tensor(act2[:, mix_tile(e), TOK:2 * TOK], pb[e % 2][:, 0:TOK],
                                      act2[:, mix_tile(e), 0:TOK].bitcast(f32), ALU.subtract)\
                       .then_inc(act2_ready, 1)

                def norm(q, shift, scale, gain, l=l):
                    dve.wait_ge(mods_done, l * BANKS + (scale + KT) // 4)
                    own.done(dve.scalar_tensor_tensor(
                        amul[:, :, :], mods[:, l, scale:scale + KT, :], 1.0,
                        vecs[:, l, 0, gain:gain + KT].unsqueeze(2).to_broadcast([P, KT, S]), ALU.add, ALU.mult))
                    dve.wait_ge(std_ready, q + 1)
                    own.link(dve.reciprocal(rstd[:, :], std[:, :]))
                    with dve.Fori(0, KT // UNROLL_K) as i:
                        for k in range(UNROLL_K):
                            for s in range(S):
                                tile = bass.ds(UNROLL_K * i + k, 1)
                                dve.scalar_tensor_tensor(
                                    ybuf[:, 2 * k + s:2 * k + s + 1, :], xT[:, tile, s * P:(s + 1) * P],
                                    amul[:, tile, s], rstd[:, s * P:(s + 1) * P].unsqueeze(1),
                                    ALU.mult, ALU.mult).then_inc(norm_y, 1)
                        for k in range(UNROLL_K):
                            for s in range(S):
                                tile = bass.ds(UNROLL_K * i + k, 1)
                                dve.wait_ge(norm_hi, q * NORM_STEPS + S * UNROLL_K * i + 2 * k + s + 1)
                                dve.scalar_tensor_tensor(
                                    hs[:, tile, TOK + s * P:TOK + (s + 1) * P], ybuf[:, 2 * k + s:2 * k + s + 1, :],
                                    mods[:, l, bass.ds(shift + UNROLL_K * i + k, 1), s],
                                    hs[:, tile, s * P:(s + 1) * P].bitcast(f32),
                                    ALU.add, ALU.subtract).then_inc(hs_ready, 1)
                        dve.wait_ge(hs_ready, q * NORM_STEPS + S * UNROLL_K * (i + 1))

                def stage(name, c, l=l):
                    if name == "norm1":
                        norm(2 * l, SHIFT1, SCALE1, V_GATTN)
                    elif name == "norm2":
                        norm(2 * l + 1, SHIFT2, SCALE2, V_GMLP)
                    elif name == "gate":
                        gate()
                    elif name == "attention":
                        attention()
                    elif name == "clear":
                        dve.memset(ssq[:, :], 0.0).then_inc(ssq_steps, 1)

                walk(dve, l, pair, stage)

            dve.wait_ge(std_ready, 2 * DEPTH + 1)
            own.link(dve.reciprocal(rstd[:, :], std[:, :]))
            for k in range(KT):
                for s in range(S):
                    dve.scalar_tensor_tensor(yT[:, k, s * P:(s + 1) * P], xT[:, k, s * P:(s + 1) * P],
                                             vecs[:, 0, 2, V_GF + k:V_GF + k + 1], rstd[:, s * P:(s + 1) * P],
                                             ALU.mult, ALU.mult).then_inc(yT_ready, 1)


def head(e):
    win, h = e >= HEADS, e % HEADS
    kv = h // GROUP
    return win, h, (QW if win else QG) + h, (KW if win else KG) + kv, (KV if win else 0) + kv


def mix_tile(e):
    return CT + e


def exps_before(l, e):
    return 5 * HEADS * l + 2 * min(e, HEADS) + 3 * max(0, e - HEADS)


def up_tiles(l, c):
    return KT * (CHUNKS * l + c)


def constants():
    out = np.zeros((P, CONSTS), np.float32)
    p = np.arange(P)
    out[:, C_ID:C_ID + P] = np.eye(P)
    out[p ^ 32, C_PERM + p] = 1.0
    n_freq = P // 4
    inv = (np.float32(10000.0) ** (-np.arange(n_freq, dtype=np.float32) / np.float32(n_freq))).astype(np.float32)
    pos = np.arange(P)
    row, col = (pos // GRID_W).astype(np.float32), (pos % GRID_W).astype(np.float32)
    ang = np.concatenate([row[:, None] * inv] * 2 + [col[:, None] * inv] * 2, axis=1).T.astype(np.float64)
    out[:, C_COS:C_COS + P] = np.cos(ang)
    out[:, C_SIN:C_SIN + P] = np.sin(ang) * np.where((p // 32) % 2 == 0, -1.0, 1.0)[:, None]
    for s in range(S):
        out[s::32, C_SEL + s] = 1.0
    return out


_INS = ["x_prompt", "x_sample", "cache_glob_k", "cache_glob_v", "cache_win_k", "cache_win_v", "c", "c_ctx",
        "w_ada", "b_ada", "g_attn", "g_mlp", "w_in", "conv_w", "conv_b", "conv_ln_g", "conv_ln_b",
        "q_norm_g", "k_norm_g", "sink", "w_out", "w_mlp1", "w_mlp2", "g_final"]
_OUTS = [("y_prompt", (1, P, D)), ("y_sample", (1, P, D))] + [
    (name, (1, DEPTH, P, KV, P)) for name in ("new_glob_k", "new_glob_v", "new_win_k", "new_win_v")]


def kernel(**inputs):
    import concourse.bacc as bacc
    from concourse.bass_utils import run_bass_kernel_spmd

    nc = bacc.Bacc("TRN2", target_bir_lowering=False, num_devices=1)
    arrays, t = {}, {}
    for name in _INS:
        a = np.ascontiguousarray(inputs[name])
        arrays[f"in_{name}"] = a
        t[name] = nc.dram_tensor(f"in_{name}", a.shape, mybir.dt.from_np(a.dtype), kind="ExternalInput").ap()
    arrays["in_consts"] = constants()
    t["consts"] = nc.dram_tensor("in_consts", (P, CONSTS), f32, kind="ExternalInput").ap()
    for name, shape in _OUTS:
        t[name] = nc.dram_tensor(f"out_{name}", shape, f32, kind="ExternalOutput").ap()
    t["y"] = (t["y_prompt"], t["y_sample"])
    build(nc, t)
    r = run_bass_kernel_spmd(nc, [arrays], core_ids=[0])
    return tuple(r.results[0][f"out_{name}"] for name, _ in _OUTS)
```
